# Optimizing a Trainium2 kernel written in Bass

```python
import math
import jax, jax.numpy as jnp
from jax import lax
import numpy as np

D_MODEL = 1024
BATCH = 1
SEQ = 256
DEPTH = 4

N_MIXERS = 3
BLK = 128
D_FF = 2816
PLE_DIM = 256
LN_EPS = 1e-5
ROPE_THETA = 10000.0
DEEPNORM_ALPHA = (2 * DEPTH) ** 0.25
DEEPNORM_BETA = (8 * DEPTH) ** -0.25
SB_HEADS = 16
SB_HEAD_DIM = 64
SWA_Q_HEADS = 16
SWA_KV_HEADS = 2
SWA_HEAD_DIM = 64
SWA_WINDOW = 128
DIL_HEADS = 16
DIL_HEAD_DIM = 64
DIL_GROUPS = ((128, 1), (512, 4), (2048, 16))
N_SB = (DEPTH + 2) // 3
N_SWA = (DEPTH + 1) // 3
N_DIL = DEPTH // 3
NEG_INF = -1e30

kernel_name = 'hybrid_interleaved_sb_swa_dilated_macaron'

def _layernorm(x, g, b):
    xf = x.astype(jnp.float32)
    mu = xf.mean(-1, keepdims=True)
    var = jnp.square(xf - mu).mean(-1, keepdims=True)
    y = (xf - mu) * lax.rsqrt(var + LN_EPS) * g.astype(jnp.float32) + b.astype(jnp.float32)
    return y.astype(x.dtype)

def _swiglu(x, w_in, w_out):
    gate, up = jnp.split(x @ w_in, 2, axis=-1)
    return (jax.nn.silu(gate) * up) @ w_out

def _rope_tables(seq, dh):
    pos = jnp.arange(seq, dtype=jnp.float32)
    inv = ROPE_THETA ** (-jnp.arange(0, dh, 2, dtype=jnp.float32) / dh)
    ang = pos[:, None] * inv[None, :]
    return jnp.cos(ang), jnp.sin(ang)

def _rope(x, cos, sin):
    xf = x.astype(jnp.float32)
    half = xf.shape[-1] // 2
    x1, x2 = xf[..., :half], xf[..., half:]
    c, s = cos[None, :, None, :], sin[None, :, None, :]
    return jnp.concatenate([x1 * c - x2 * s, x2 * c + x1 * s], axis=-1).astype(x.dtype)

def _banded_attention(q, k, v, max_dist, sinks):
    bsz, L, hq, dh = q.shape
    hk = k.shape[2]
    g = hq // hk
    lp = -(-L // BLK) * BLK
    pad = ((0, 0), (0, lp - L), (0, 0), (0, 0))
    nb = lp // BLK
    qb = jnp.pad(q, pad).astype(jnp.float32).reshape(bsz, nb, BLK, hk, g, dh)
    kb = jnp.pad(k, pad).astype(jnp.float32).reshape(bsz, nb, BLK, hk, dh)
    vb = jnp.pad(v, pad).astype(jnp.float32).reshape(bsz, nb, BLK, hk, dh)
    prev = ((0, 0), (1, 0), (0, 0), (0, 0), (0, 0))
    kk = jnp.concatenate([jnp.pad(kb, prev)[:, :-1], kb], axis=2)
    vv = jnp.concatenate([jnp.pad(vb, prev)[:, :-1], vb], axis=2)
    s = jnp.einsum('bnqhgd,bnkhd->bnhgqk', qb, kk) * (dh ** -0.5)
    qi = jnp.arange(BLK)[:, None]
    kj = jnp.arange(2 * BLK)[None, :]
    diff = BLK + qi - kj
    blk = jnp.arange(nb)[:, None, None]
    valid = (diff >= 0) & (diff <= max_dist) & ((blk > 0) | (kj >= BLK))
    s = jnp.where(valid[None, :, None, None], s, NEG_INF)
    m = s.max(-1)
    if sinks is not None:
        sink = sinks.astype(jnp.float32).reshape(hk, g)[None, None, :, :, None]
        m = jnp.maximum(m, sink)
        e = jnp.exp(s - m[..., None])
        den = e.sum(-1) + jnp.exp(sink - m)
    else:
        e = jnp.exp(s - m[..., None])
        den = e.sum(-1)
    lse = m + jnp.log(den)
    o = jnp.einsum('bnhgqk,bnkhd->bnqhgd', e / den[..., None], vv)
    o = o.reshape(bsz, lp, hq, dh)[:, :L]
    lse = lse.transpose(0, 1, 4, 2, 3).reshape(bsz, lp, hq)[:, :L]
    return o, lse

def _stick_breaking(q, k, v):
    bsz, S, H, dh = q.shape
    sp_len = -(-S // BLK) * BLK
    nb = sp_len // BLK
    qb = jnp.pad(q, ((0, 0), (0, sp_len - S), (0, 0), (0, 0))).astype(jnp.float32)
    qb = qb.reshape(bsz, nb, BLK, H, dh).transpose(1, 0, 3, 2, 4)
    kf = k.astype(jnp.float32)
    vf = v.astype(jnp.float32)
    kpos = jnp.arange(S)

    def block(args):
        qblk, n = args
        z = jnp.einsum('bhqd,bshd->bhqs', qblk, kf) * (dh ** -0.5)
        qpos = n * BLK + jnp.arange(BLK)
        causal = kpos[None, :] < qpos[:, None]
        sp = jnp.where(causal, jax.nn.softplus(z), 0.0)
        after = lax.cumsum(sp, axis=3, reverse=True) - sp
        a = jnp.where(causal, jnp.exp(jax.nn.log_sigmoid(z) - after), 0.0)
        return jnp.einsum('bhqs,bshd->bqhd', a, vf)

    o = lax.map(block, (qb, jnp.arange(nb)))
    return o.transpose(1, 0, 2, 3, 4).reshape(bsz, sp_len, H, dh)[:, :S].astype(q.dtype)

def _sb_mixer(x, w_in, w_out):
    bsz, S, _ = x.shape
    h = (x @ w_in).reshape(bsz, S, 3, SB_HEADS, SB_HEAD_DIM)
    o = _stick_breaking(h[:, :, 0], h[:, :, 1], h[:, :, 2])
    return o.reshape(bsz, S, SB_HEADS * SB_HEAD_DIM) @ w_out

def _swa_mixer(x, w_in, sinks, w_out, cos, sin):
    bsz, S, _ = x.shape
    nq = SWA_Q_HEADS * SWA_HEAD_DIM
    nkv = SWA_KV_HEADS * SWA_HEAD_DIM
    h = x @ w_in
    q = _rope(h[..., :nq].reshape(bsz, S, SWA_Q_HEADS, SWA_HEAD_DIM), cos, sin)
    k = _rope(h[..., nq:nq + nkv].reshape(bsz, S, SWA_KV_HEADS, SWA_HEAD_DIM), cos, sin)
    v = h[..., nq + nkv:].reshape(bsz, S, SWA_KV_HEADS, SWA_HEAD_DIM)
    o, _ = _banded_attention(q, k, v, SWA_WINDOW - 1, sinks)
    return o.reshape(bsz, S, nq).astype(x.dtype) @ w_out

def _dilated_mixer(x, w_in, w_out, cos, sin):
    bsz, S, _ = x.shape
    h = (x @ w_in).reshape(bsz, S, len(DIL_GROUPS), 3, DIL_HEADS, DIL_HEAD_DIM)
    outs, lses = [], []
    for gi, (win, dil) in enumerate(DIL_GROUPS):
        q = _rope(h[:, :, gi, 0], cos, sin)
        k = _rope(h[:, :, gi, 1], cos, sin)
        v = h[:, :, gi, 2]
        sp_len = -(-S // dil) * dil
        ls = sp_len // dil

        def strided(a):
            a = jnp.pad(a, ((0, 0), (0, sp_len - S), (0, 0), (0, 0)))
            return a.reshape(bsz, ls, dil, DIL_HEADS, DIL_HEAD_DIM).transpose(0, 2, 1, 3, 4).reshape(
                bsz * dil, ls, DIL_HEADS, DIL_HEAD_DIM)

        o, lse = _banded_attention(strided(q), strided(k), strided(v), win // dil, None)
        o = o.reshape(bsz, dil, ls, DIL_HEADS, DIL_HEAD_DIM).transpose(0, 2, 1, 3, 4).reshape(
            bsz, sp_len, DIL_HEADS, DIL_HEAD_DIM)[:, :S]
        lse = lse.reshape(bsz, dil, ls, DIL_HEADS).transpose(0, 2, 1, 3).reshape(bsz, sp_len, DIL_HEADS)[:, :S]
        outs.append(o)
        lses.append(lse)
    w = jax.nn.softmax(jnp.stack(lses), axis=0)
    o = jnp.einsum('gbsh,gbshd->bshd', w, jnp.stack(outs))
    return o.reshape(bsz, S, DIL_HEADS * DIL_HEAD_DIM).astype(x.dtype) @ w_out

def setup_inputs(seed: int = 0) -> dict:
    key = jax.random.key(seed)
    ks = jax.random.split(key, 18)
    f32 = jnp.float32

    def nrm(k, shape, scale):
        return jax.random.normal(k, shape, f32) * scale

    sb_w = SB_HEADS * SB_HEAD_DIM
    swa_in = (SWA_Q_HEADS + 2 * SWA_KV_HEADS) * SWA_HEAD_DIM
    swa_w = SWA_Q_HEADS * SWA_HEAD_DIM
    dil_in = len(DIL_GROUPS) * 3 * DIL_HEADS * DIL_HEAD_DIM
    dil_w = DIL_HEADS * DIL_HEAD_DIM
    return {
        'x': nrm(ks[0], (BATCH, SEQ, D_MODEL), 1.0),
        'p': nrm(ks[1], (DEPTH, BATCH, SEQ, PLE_DIM), 1.0),
        'ffn1_w_in': nrm(ks[2], (DEPTH, D_MODEL, 2 * D_FF), D_MODEL ** -0.5),
        'ffn1_w_out': nrm(ks[3], (DEPTH, D_FF, D_MODEL), D_FF ** -0.5 * DEEPNORM_BETA),
        'ffn2_w_in': nrm(ks[4], (DEPTH, D_MODEL, 2 * D_FF), D_MODEL ** -0.5),
        'ffn2_w_out': nrm(ks[5], (DEPTH, D_FF, D_MODEL), D_FF ** -0.5 * DEEPNORM_BETA),
        'ln_g': 1.0 + nrm(ks[6], (DEPTH, 3, D_MODEL), 0.02),
        'ln_b': nrm(ks[7], (DEPTH, 3, D_MODEL), 0.02),
        'sb_w_in': nrm(ks[8], (N_SB, D_MODEL, 3 * sb_w), D_MODEL ** -0.5),
        'sb_w_out': nrm(ks[9], (N_SB, sb_w, D_MODEL), sb_w ** -0.5 * DEEPNORM_BETA),
        'swa_w_in': nrm(ks[10], (N_SWA, D_MODEL, swa_in), D_MODEL ** -0.5),
        'swa_sinks': nrm(ks[11], (N_SWA, SWA_Q_HEADS), 0.5),
        'swa_w_out': nrm(ks[12], (N_SWA, swa_w, D_MODEL), swa_w ** -0.5 * DEEPNORM_BETA),
        'dil_w_in': nrm(ks[13], (N_DIL, D_MODEL, dil_in), D_MODEL ** -0.5),
        'dil_w_out': nrm(ks[14], (N_DIL, dil_w, D_MODEL), dil_w ** -0.5 * DEEPNORM_BETA),
        'ple_w_proj': nrm(ks[15], (DEPTH, PLE_DIM, D_MODEL), PLE_DIM ** -0.5),
        'ple_w_gate': nrm(ks[16], (DEPTH, D_MODEL, D_MODEL), D_MODEL ** -0.5),
    }

def reference(x, p, ffn1_w_in, ffn1_w_out, ffn2_w_in, ffn2_w_out, ln_g, ln_b,
              sb_w_in, sb_w_out, swa_w_in, swa_sinks, swa_w_out, dil_w_in, dil_w_out,
              ple_w_proj, ple_w_gate):
    S = x.shape[1]
    cos, sin = _rope_tables(S, SWA_HEAD_DIM)
    a = DEEPNORM_ALPHA
    for i in range(DEPTH):
        kind, j = i % N_MIXERS, i // N_MIXERS
        x = _layernorm(a * x + 0.5 * _swiglu(x, ffn1_w_in[i], ffn1_w_out[i]), ln_g[i, 0], ln_b[i, 0])
        if kind == 0:
            mix = _sb_mixer(x, sb_w_in[j], sb_w_out[j])
        elif kind == 1:
            mix = _swa_mixer(x, swa_w_in[j], swa_sinks[j], swa_w_out[j], cos, sin)
        else:
            mix = _dilated_mixer(x, dil_w_in[j], dil_w_out[j], cos, sin)
        x = _layernorm(a * x + mix, ln_g[i, 1], ln_b[i, 1])
        x = _layernorm(a * x + 0.5 * _swiglu(x, ffn2_w_in[i], ffn2_w_out[i]), ln_g[i, 2], ln_b[i, 2])
        x = x + jax.nn.sigmoid(x @ ple_w_gate[i]) * (p[i] @ ple_w_proj[i])
    return x


_drawn_inputs = setup_inputs


def setup_inputs(seed=0):
    import zlib

    import numpy as np

    out = dict(_drawn_inputs(seed))
    spreads = {}
    factors = {'swa_sinks': 24.833}
    for name, (base, spread) in spreads.items():
        noise = np.random.default_rng([zlib.crc32(name.encode()), seed]).standard_normal(out[name].shape)
        drawn = base * np.exp(spread * noise) if base else spread * noise
        out[name] = __import__('jax').numpy.asarray(drawn.astype(out[name].dtype))
    for name, factor in factors.items():
        out[name] = (out[name] * factor).astype(out[name].dtype)
    return out
```

```python
from contextlib import ExitStack

import concourse.bass as bass
from concourse import mybir

F32 = mybir.dt.float32
F32R = mybir.dt.float32r
I32 = mybir.dt.int32
ALU = mybir.AluOpType
ACT = mybir.ActivationFunctionType

P = 128
D = 1024
S = 256
NT = S // P
DEPTH = 4
FF = 2816
PLE = 256
HD = 64
HALF = 8
ALPHA = (2 * DEPTH) ** 0.25
EPS = 1e-5
NEG = -1e30
RING = 6
LEAD = 4
UW = 1024
BLK = 512
NJ = FF // BLK
DIL = ((128, 1), (512, 4), (2048, 16))
NG = len(DIL)

CONST = {}
_at = 0
for _name, _n in (("ident", P), ("lower", P), ("ones", P), ("keep", P), ("kill", P), ("swa", 3 * P),
                  ("dil", 3 * NG * P), ("cq", 64), ("sq", 64), ("nsq", 64), ("ck", 64), ("sk", 64), ("nsk", 64),
                  ("sink", 16)):
    CONST[_name] = (_at, _at + _n)
    _at += _n
CONST_W = _at


def mixer_of(l):
    return ("sb", "swa", "dil")[l % 3]


class Signal:

    def __init__(self, sem):
        self.sem, self.place = sem, {}

    def note(self, *key):
        self.place[key] = len(self.place) + 1

    def at(self, *key):
        return self.place[key]


def triples_of(l):
    kind = mixer_of(l)
    if kind == "swa":
        return [("q", 0, 0), ("kv", 0, 0), ("attn", 0, 0), ("q", 1, 0), ("attn", 1, 0)]
    steps = []
    for hh in range(2):
        for g in range(NG if kind == "dil" else 1):
            steps += [("q", hh, g), ("k", hh, g), ("v", hh, g)]
        steps.append(("attn", hh, 0))
    return steps


def units_of(step):
    return 2 if step == "kv" else 4


def build_program(nc, A, out):
    ctx = ExitStack()
    with ctx:
        def sb(name, shape, dt=F32):
            return ctx.enter_context(nc.sbuf_tensor(name, shape, dt))

        raw = sb("raw", [P, RING, UW])
        wh = sb("wh", [P, RING, UW], F32R)
        wl = sb("wl", [P, RING, UW], F32R)
        x = sb("x", [P, NT, D])
        xh = sb("xh", [P, D // P, NT, P], F32R)
        xl = sb("xl", [P, D // P, NT, P], F32R)
        hth = sb("hth", [P, 6, NT, P], F32R)
        htl = sb("htl", [P, 6, NT, P], F32R)
        pth = sb("pth", [P, 2, NT, P], F32R)
        ptl = sb("ptl", [P, 2, NT, P], F32R)
        pin = sb("pin", [P, NT, PLE])
        gb = sb("gb", [P, 2, D])
        consts = sb("consts", [P, CONST_W])
        stats = sb("stats", [P, NT, 2, 6])
        mv = sb("mv", [P, NT, 2])
        veps = sb("veps", [P, NT, 1])
        rstd = sb("rstd", [P, NT, 1])
        mhalf = sb("mhalf", [P, 1])
        nmx = sb("nmx", [P, 3, 16])
        arena = sb("arena", [P, 16384])
        place = [0]

        def part(n):
            place[0] += n
            return arena[:, place[0] - n:place[0]]

        qT = part(NG * 4 * S).rearrange("p (g c s) -> p g c s", g=NG, c=4)
        kT = part(NG * 4 * S).rearrange("p (g c s) -> p g c s", g=NG, c=4)
        vv = part(NG * NT * BLK).rearrange("p (g t n) -> p g t n", g=NG, t=NT)
        qk = part(NT * BLK).rearrange("p (t n) -> p t n", t=NT)
        ra = part(BLK)
        rb = part(BLK)
        sc = part(2 * 768).rearrange("p (b n) -> p b n", b=2)
        eT = part(2 * 768).rearrange("p (b m q) -> p b m q", b=2, m=6)
        o = part(NT * D).rearrange("p (t n) -> p t n", t=NT)
        sg = arena[:, 0:NT * BLK].rearrange("p (t n) -> p t n", t=NT)
        hb = arena[:, NT * BLK:2 * NT * BLK].rearrange("p (t n) -> p t n", t=NT)
        eg = arena[:, 0:NT * D].rearrange("p (t n) -> p t n", t=NT)
        sw = sc
        ssp = eT.rearrange("p b m q -> p b (m q)")[:, :, 0:384]
        sa = eT.rearrange("p b m q -> p b (m q)")[:, :, 384:768]

        ps = ctx.enter_context(nc.psum_tensor("ps", [P, 8, BLK], F32))

        def const(name):
            a, b = CONST[name]
            return consts[:, a:b]

        ident = const("ident")

        def signal(name):
            return Signal(ctx.enter_context(nc.semaphore(name)))

        def semaphore(name):
            return ctx.enter_context(nc.semaphore(name))

        landed = [semaphore(f"landed{s}") for s in range(RING)]
        hi_done = semaphore("hi_done")
        lo_done = semaphore("lo_done")
        w_used = semaphore("w_used")
        x_landed = semaphore("x_landed")
        c_landed = semaphore("c_landed")
        g_landed = semaphore("g_landed")
        b_landed = semaphore("b_landed")
        p_landed = semaphore("p_landed")
        stored = [semaphore(f"stored{t}") for t in range(NT)]
        acc_ready = signal("acc_ready")
        t_ready = signal("t_ready")
        th_done = signal("th_done")
        tl_done = signal("tl_done")
        silu_done = signal("silu_done")
        h_done = signal("h_done")
        x_new = signal("x_new")
        var_done = signal("var_done")
        rstd_done = signal("rstd_done")
        tok_done = signal("tok_done")
        v_done = signal("v_done")
        s_done = signal("s_done")
        e_done = signal("e_done")
        eT0_done = signal("eT0_done")
        eT1_done = signal("eT1_done")
        sk_done = signal("sk_done")
        ln_done = signal("ln_done")
        sp_done = signal("sp_done")
        cum_done = signal("cum_done")
        dm_done = signal("dm_done")
        a_done = signal("a_done")
        o_done = signal("o_done")
        sig_done = signal("sig_done")
        own_act = semaphore("own_act")
        own_dve = semaphore("own_dve")
        mh_done = semaphore("mh_done")

        stages = []
        u = 0
        for l in range(DEPTH):
            for kind in ("ffn1", "mix", "ffn2", "ple"):
                n = {"ffn1": 66, "ffn2": 66, "ple": 10, "mix": 8 + sum(units_of(s[0]) for s in triples_of(l) if s[0] != "attn")}[kind]
                stages.append((kind, l, len(stages), u, n))
                u += n
        UNITS = u
        NST = len(stages)

        ends = {}
        for t in range(NT):
            t_ready.note("x", 0, t), th_done.note("x", 0, t), tl_done.note("x", 0, t)
        for kind, l, i, u0, n in stages:
            if kind in ("ffn1", "ffn2"):
                for j in range(NJ + 1):
                    base = u0 if j == 0 else u0 + 8 + 12 * (j - 1)
                    ends["gate", i, j] = base + (4 if j < NJ else 2)
                    ends["up", i, j] = base + (8 if j == 0 else 12 if j < NJ else 4)
                    silu_done.note(i, j), h_done.note(i, j)
                    t_ready.note("h", i, j), th_done.note("h", i, j), tl_done.note("h", i, j)
            elif kind == "mix":
                at = u0
                for what, hh, g in triples_of(l):
                    if what != "attn":
                        at += units_of(what)
                        ends[what, i, hh, g] = at
                        if what != "v":
                            tok_done.note(what, i, hh, g)
                            t_ready.note(what, i, hh, g), th_done.note(what, i, hh, g)
                        if what in ("v", "kv"):
                            v_done.note(i, hh, g)
                    elif mixer_of(l) == "sb":
                        for h in range(HALF):
                            for sg_, pre in ((acc_ready, "z"), (ln_done, "l"), (sp_done, "s"), (cum_done, "c"), (dm_done, "d"), (a_done, "a")):
                                sg_.note(pre, i, hh, h)
                        acc_ready.note("o", i, hh), o_done.note(i, hh)
                    else:
                        for h in range(HALF):
                            for t in range(NT):
                                acc_ready.note("z", i, hh, h, t), s_done.note(i, hh, h, t), e_done.note(i, hh, h, t)
                                t_ready.note("e", i, hh, h, t)
                                (eT0_done, eT1_done)[t].note(i, hh, h)
                        if mixer_of(l) == "swa":
                            sk_done.note(i, hh)
                        acc_ready.note("o", i, hh), o_done.note(i, hh)
                for t in range(NT):
                    t_ready.note("o", i, t), th_done.note("o", i, t), tl_done.note("o", i, t)
            else:
                ends["gate", i] = u0 + 8
                t_ready.note("p", i), th_done.note("p", i), tl_done.note("p", i), sig_done.note(i)
            ends["y", i] = u0 + n
            for t in range(NT):
                if t == 0:
                    acc_ready.note("y", i)
                x_new.note(i, t)
                if kind != "ple":
                    var_done.note(i, t), rstd_done.note(i, t)
                if i + 1 < NST:
                    t_ready.note("x", i + 1, t), th_done.note("x", i + 1, t), tl_done.note("x", i + 1, t)

        norm_index = {i: 3 * l + ("ffn1", "mix", "ffn2").index(kind) for kind, l, i, _, _ in stages if kind != "ple"}

        def wait(eng, sig, *key):
            eng.wait_ge(sig.sem, sig.at(*key))

        def cells(slot, n):
            return slice(0, UW), n

        def view(ring, slot, ncol):
            return ring[:, slot, :].rearrange("p (k n) -> p k n", n=ncol)

        block = ctx.enter_context(nc.Block())

        @block.sync
        def _(sp):
            st = {"u": 0}

            def load(src, rows, cols, ncol, base=None):
                u = st["u"]
                st["u"] += 1
                lo = 0 if base is None else base
                if u >= RING:
                    sp.wait_ge(lo_done, u - RING + 1 + lo)
                nk = UW // ncol
                v = src.rearrange("(k p) n -> p k n", p=P)
                sp.dma_start(view(raw, u % RING, ncol),
                             v[:, bass.ds(rows, nk), bass.ds(cols, ncol)]).then_inc(landed[u % RING], 16)

            def ffn(l, i, win, wout):
                def block_of(j, base, first=False):
                    for k in range(0, 8, 2):
                        load(win, k, j * BLK, BLK, base)
                    if not first:
                        for k in range(2):
                            for c in range(2):
                                load(wout, j * 4 - 4 + 2 * k, c * BLK, BLK, base)
                    for k in range(0, 8, 2):
                        load(win, k, j * BLK + FF, BLK, base)
                block_of(0, None, True)
                norm_load(i)
                with sp.Fori(0, NJ - 1) as r:
                    block_of(r + 1, r * 12)
                st["u"] += 12 * (NJ - 2)
                for c in (NJ * BLK, NJ * BLK + FF):
                    for k in (0, 4):
                        load(win, k, c, 256)
                for k in range(3):
                    for c in range(2):
                        load(wout, NJ * 4 - 4 + 2 * k, c * BLK, BLK)

            def norm_load(i):
                n = norm_index[i]
                if n:
                    before = i - 1 if i - 1 in norm_index else i - 2
                    wait(sp, x_new, before, 1)
                if True:
                    sp.dma_start(gb[:, 0, :], A["ln_g"].rearrange("l k n -> (l k) n")[n].partition_broadcast(P)).then_inc(g_landed, 16)
                    sp.dma_start(gb[:, 1, :], A["ln_b"].rearrange("l k n -> (l k) n")[n].partition_broadcast(P)).then_inc(b_landed, 16)

            sp.dma_start(x[:], A["x"][0].rearrange("(t p) n -> p t n", p=P)).then_inc(x_landed, 16)
            sp.dma_start(consts[:, 0:CONST["sink"][0]], A["consts"]).then_inc(c_landed, 16)
            sp.dma_start(const("sink"), A["swa_sinks"][0].partition_broadcast(P)).then_inc(p_landed, 16)
            for kind, l, i, u0, n in stages:
                assert st["u"] == u0, (kind, st["u"], u0)
                if kind == "ffn1":
                    ffn(l, i, A["ffn1_w_in"][l], A["ffn1_w_out"][l])
                elif kind == "ffn2":
                    ffn(l, i, A["ffn2_w_in"][l], A["ffn2_w_out"][l])
                elif kind == "mix":
                    name = mixer_of(l)
                    win, wout = A[f"{name}_w_in"][l // 3], A[f"{name}_w_out"][l // 3]
                    for n, (what, hh, g) in enumerate(triples_of(l)):
                        if n == 2:
                            norm_load(i)
                        if what == "kv":
                            for k in (0, 4):
                                load(win, k, D, 256)
                        elif what != "attn":
                            col = g * 3 * D + "qkv".index(what) * D + hh * BLK
                            for k in range(0, 8, 2):
                                load(win, k, col, BLK)
                    for k in range(0, 8, 2):
                        for c in range(2):
                            load(wout, k, c * BLK, BLK)
                else:
                    if l:
                        wait(sp, t_ready, "p", i - 4)
                    sp.dma_start(pin[:], A["p"][l, 0].rearrange("(t p) n -> p t n", p=P)).then_inc(p_landed, 16)
                    for k in range(0, 8, 2):
                        for c in range(2):
                            load(A["ple_w_gate"][l], k, c * BLK, BLK)
                    for c in range(2):
                        load(A["ple_w_proj"][l], 0, c * BLK, BLK)
            for t in range(NT):
                wait(sp, x_new, NST - 1, t)
                sp.dma_start(out[0].rearrange("(t p) n -> p t n", p=P)[:, t, :], x[:, t, :]).then_inc(stored[t], 16)
            for t in range(NT):
                sp.wait_ge(stored[t], 16)

        @block.gpsimd
        def _(pool):
            pool.memset(mhalf[:], -0.5).then_inc(mh_done, 1)
            pool.wait_ge(mh_done, 1)
            for kind, l, i, u0, n in stages:
                if kind != "ple":
                    for t in range(NT):
                        wait(pool, var_done, i, t)
                        pool.tensor_tensor(rstd[:, t, :], veps[:, t, :], mhalf[:], ALU.pow).then_inc(rstd_done.sem, 1)

        @block.scalar
        def _(act):
            st = {"u": 0, "own": 0}

            def own(ins):
                st["own"] += 1
                ins.then_inc(own_act, 1)
                act.wait_ge(own_act, st["own"])

            def split(n=1, loop=None):
                for _ in range(n):
                    u = st["u"]
                    if u >= UNITS:
                        return
                    st["u"] += 1
                    du, dr = loop or (0, 0)
                    act.wait_ge(landed[u % RING], 16 * (u // RING + 1) + dr)
                    if u >= RING:
                        act.wait_ge(w_used, u - RING + 1 + du)
                    act.activation(wh[:, u % RING, :], raw[:, u % RING, :], ACT.Copy).then_inc(hi_done, 1)

            def t_high(dst, bank, key, cols=BLK, nb=2, first_bank=None):
                pass

            def stream_t(key, i, t):
                wait(act, t_ready, key, i, t)
                for q in range(2):
                    ins = act.activation(xh[:, 4 * q:4 * q + 4, t, :], ps[:, 2 * t + q, :].rearrange("p (c m) -> p c m", m=P), ACT.Copy)
                ins.then_inc(th_done.sem, 1)

            def hidden_t(i, j, n, at, dj=0):
                act.wait_ge(t_ready.sem, t_ready.at("h", i, j) + dj)
                for t in range(NT):
                    ins = act.activation(hth[:, at:at + n, t, :], ps[:, 2 + t, 0:n * P].rearrange("p (c m) -> p c m", m=P), ACT.Copy)
                ins.then_inc(th_done.sem, 1)

            def silu(i, j, n, dj=0):
                act.wait_ge(w_used, ends["gate", i, j] + 12 * dj)
                for t in range(NT):
                    ins = act.activation(sg[:, t, 0:n], ps[:, t, 0:n], ACT.Silu)
                ins.then_inc(silu_done.sem, 1)

            def ffn(i):
                split(8 - 4)
                silu(i, 0, BLK)
                split(4)
                with act.Fori(0, NJ - 1) as r:
                    lp = (r * 12, r * 32)
                    split(3, lp)
                    hidden_t(i, 0, 4, 0, r)
                    split(2, lp)
                    silu(i, 1, BLK, r)
                    split(7, lp)
                st["u"] += 12 * (NJ - 2)
                split(2)
                hidden_t(i, NJ - 1, 4, 0)
                silu(i, NJ, 256)
                split(4)
                hidden_t(i, NJ, 2, 4)

            def boundary(i, last=False):
                for t in range(NT):
                    if i + 1 < NST:
                        if t == 0:
                            split(1)
                        stream_t("x", i + 1, t)
                        if t == 0:
                            split(1)

            def copy_t(what, i, hh, g, dst):
                wait(act, t_ready, what, i, hh, g)
                n = 2 if what == "kv" else 4
                for t in range(NT):
                    ins = act.activation(dst[:, g, 0:n, t * P:(t + 1) * P],
                                         ps[:, 4 + t, 0:n * P].rearrange("p (c m) -> p c m", m=P), ACT.Copy)
                ins.then_inc(th_done.sem, 1)

            def softmax_half(kind, i, hh):
                ng = NG if kind == "dil" else 1

                def exps(h, t):
                    n = 2 * h + t
                    wait(act, s_done, i, hh, h, t)
                    w = (t + 1) * ng * P
                    act.activation(sc[:, n % 2, 0:w], sc[:, n % 2, 0:w], ACT.Exp, bias=nmx[:, 1, t * 8 + h:t * 8 + h + 1],
                                   accum_out=nmx[:, 2, t * 8 + h:t * 8 + h + 1]).then_inc(e_done.sem, 1)

                def evac0(h):
                    wait(act, t_ready, "e", i, hh, h, 0)
                    act.activation(eT[:, 0, 0:ng, :], ps[:, 6, 0:ng * P].rearrange("p (c m) -> p c m", m=P),
                                   ACT.Copy).then_inc(eT0_done.sem, 1)
                exps(0, 0)
                for h in range(HALF):
                    exps(h, 1)
                    evac0(h)
                    if h + 1 < HALF:
                        exps(h + 1, 0)
                if kind == "swa":
                    for t in range(NT):
                        for h in range(HALF):
                            c = t * 8 + h
                            ins = act.activation(nmx[:, 0, c:c + 1], const("sink")[:, hh * 8 + h:hh * 8 + h + 1], ACT.Exp,
                                                 bias=nmx[:, 1, c:c + 1])
                    ins.then_inc(sk_done.sem, 1)

            def stick_half(i, hh):
                def logs(h):
                    wait(act, acc_ready, "z", i, hh, h)
                    if h >= 2:
                        wait(act, sp_done, "s", i, hh, h - 2)
                    w = sw[:, h % 2, 0:384]
                    own(act.activation(w, ps[:, h % 4, 0:384], ACT.Abs))
                    own(act.activation(w, w, ACT.Exp, scale=-1.0))
                    act.activation(w, w, ACT.Ln, bias=1.0).then_inc(ln_done.sem, 1)

                def weights(h):
                    wait(act, dm_done, "d", i, hh, h)
                    a = sa[:, h % 2, :]
                    act.activation(a[:, P:2 * P], ps[:, h % 4, P:2 * P], ACT.Exp)
                    dg = a.rearrange("p (m q) -> p m q", m=3)[:, 0:3:2, :]
                    act.activation(dg, dg, ACT.Exp).then_inc(a_done.sem, 1)
                logs(0)
                for h in range(HALF):
                    if h + 1 < HALF:
                        logs(h + 1)
                    weights(h)

            def mix(l, i):
                kind = mixer_of(l)
                late = []
                for n, (what, hh, g) in enumerate(triples_of(l)):
                    if what == "attn":
                        for f in late:
                            f()
                        late = []
                        if n == 2 and kind == "swa":
                            pass
                        stick_half(i, hh) if kind == "sb" else softmax_half(kind, i, hh)
                        continue
                    nu = units_of(what)
                    split(nu - 1)
                    for f in late:
                        f()
                    late = []
                    split(1)
                    if what != "v":
                        late = [lambda what=what, hh=hh, g=g: copy_t(what, i, hh, g, qT if what == "q" else kT)]
                stream_t("o", i, 0)
                stream_t("o", i, 1)
                split(4)

            def ple(i):
                split(2)
                wait(act, t_ready, "p", i)
                act.activation(pth[:], ps[:, 0, :].rearrange("p (c t m) -> p c t m", c=2, t=NT), ACT.Copy).then_inc(th_done.sem, 1)
                split(4)
                act.wait_ge(w_used, ends["gate", i])
                for t in range(NT):
                    ins = act.activation(eg[:, t, :], ps[:, 4 + 2 * t:6 + 2 * t, :].rearrange("p c n -> p (c n)"), ACT.Sigmoid)
                ins.then_inc(sig_done.sem, 1)

            split(LEAD)
            for t in range(NT):
                stream_t("x", 0, t)
            for kind, l, i, u0, n in stages:
                assert st["u"] == u0 + LEAD, (kind, st["u"], u0)
                if kind in ("ffn1", "ffn2"):
                    ffn(i)
                elif kind == "mix":
                    mix(l, i)
                else:
                    ple(i)
                split(2)
                boundary(i)

        @block.vector
        def _(dve):
            st = {"u": 0, "own": 0}

            def own(ins):
                st["own"] += 1
                ins.then_inc(own_dve, 1)
                dve.wait_ge(own_dve, st["own"])

            def split(n=1, du=0):
                for _ in range(n):
                    u = st["u"]
                    if u >= UNITS:
                        return
                    st["u"] += 1
                    dve.wait_ge(hi_done, u + 1 + du)
                    dve.tensor_tensor(wl[:, u % RING, :], raw[:, u % RING, :], wh[:, u % RING, :].bitcast(F32),
                                      ALU.subtract).then_inc(lo_done, 1)

            def stream_t(key, i, t):
                wait(dve, th_done, key, i, t)
                for q in range(2):
                    ins = dve.tensor_tensor(xl[:, 4 * q:4 * q + 4, t, :], ps[:, 2 * t + q, :].rearrange("p (c m) -> p c m", m=P),
                                            xh[:, 4 * q:4 * q + 4, t, :].bitcast(F32), ALU.subtract)
                ins.then_inc(tl_done.sem, 1)

            def hidden_t(i, j, n, at, dj=0):
                dve.wait_ge(th_done.sem, th_done.at("h", i, j) + dj)
                for t in range(NT):
                    ins = dve.tensor_tensor(htl[:, at:at + n, t, :], ps[:, 2 + t, 0:n * P].rearrange("p (c m) -> p c m", m=P),
                                            hth[:, at:at + n, t, :].bitcast(F32), ALU.subtract)
                ins.then_inc(tl_done.sem, 1)

            def hidden(i, j, n, dj=0):
                dve.wait_ge(silu_done.sem, silu_done.at(i, j) + dj)
                dve.wait_ge(w_used, ends["up", i, j] + 12 * dj)
                for t in range(NT):
                    ins = dve.scalar_tensor_tensor(hb[:, t, 0:n], sg[:, t, 0:n], 0.5, ps[:, 2 + t, 0:n], ALU.mult, ALU.mult)
                ins.then_inc(h_done.sem, 1)

            def ffn(i):
                split(8)
                hidden(i, 0, BLK)
                with dve.Fori(0, NJ - 1) as r:
                    split(3, r * 12)
                    hidden_t(i, 0, 4, 0, r)
                    split(9, r * 12)
                    hidden(i, 1, BLK, r)
                st["u"] += 12 * (NJ - 2)
                split(2)
                hidden_t(i, NJ - 1, 4, 0)
                split(2)
                hidden(i, NJ, 256)
                split(2)
                hidden_t(i, NJ, 2, 4)

            def y_wait(i, t):
                wait(dve, acc_ready, "y", i) if t == 0 else dve.wait_ge(w_used, ends["y", i])

            def norm(i, t):
                y_wait(i, t)
                for c in range(2):
                    ins = dve.scalar_tensor_tensor(x[:, t, c * BLK:(c + 1) * BLK], x[:, t, c * BLK:(c + 1) * BLK], ALPHA,
                                                   ps[:, 4 + 2 * t + c, :], ALU.mult, ALU.add)
                own(ins)
                for c in range(2):
                    ins = dve.bn_stats(stats[:, t, c, :], x[:, t, c * BLK:(c + 1) * BLK])
                own(ins)
                own(dve.bn_aggr(mv[:, t, :], stats[:, t, :, :]))
                dve.tensor_scalar_add(veps[:, t, :], mv[:, t, 1:2], EPS).then_inc(var_done.sem, 1)
                if t == 0:
                    dve.wait_ge(g_landed, 16 * (norm_index[i] + 1))
                    dve.wait_ge(b_landed, 16 * (norm_index[i] + 1))
                own(dve.scalar_tensor_tensor(x[:, t, :], x[:, t, :], mv[:, t, 0:1], gb[:, 0, :], ALU.subtract, ALU.mult))
                wait(dve, rstd_done, i, t)
                dve.scalar_tensor_tensor(x[:, t, :], x[:, t, :], rstd[:, t, :], gb[:, 1, :], ALU.mult, ALU.add).then_inc(x_new.sem, 1)

            def embed(i, t):
                if t == 0:
                    wait(dve, sig_done, i)
                y_wait(i, t)
                own(dve.tensor_tensor(eg[:, t, :], eg[:, t, :], ps[:, 2 * t:2 * t + 2, :].rearrange("p c n -> p (c n)"), ALU.mult))
                dve.tensor_tensor(x[:, t, :], x[:, t, :], eg[:, t, :], ALU.add).then_inc(x_new.sem, 1)

            def boundary(kind, i):
                for t in range(NT):
                    (embed if kind == "ple" else norm)(i, t)
                    if i + 1 < NST:
                        if t == 0:
                            split(1)
                        stream_t("x", i + 1, t)
                        if t == 0:
                            split(1)

            def rotate(dst, bank, n, cs, t):
                c, s, ns = (const(k)[:, t * 32:(t + 1) * 32].unsqueeze(1).broadcast_to((P, n, 32)) for k in cs)
                v = ps[:, bank, 0:n * HD].rearrange("p (h w d) -> p h w d", w=2, d=32)
                a = ra[:, 0:n * HD].rearrange("p (h w d) -> p h w d", w=2, d=32)
                b = rb[:, 0:n * HD].rearrange("p (h w d) -> p h w d", w=2, d=32)
                for w in range(2):
                    dve.tensor_tensor(a[:, :, w, :], v[:, :, w, :], c, ALU.mult)
                dve.tensor_tensor(b[:, :, 0, :], v[:, :, 1, :], ns, ALU.mult)
                own(dve.tensor_tensor(b[:, :, 1, :], v[:, :, 0, :], s, ALU.mult))
                for d in dst:
                    ins = dve.tensor_tensor(d, ra[:, 0:n * HD].rearrange("p (h d) -> p h d", d=HD),
                                            rb[:, 0:n * HD].rearrange("p (h d) -> p h d", d=HD), ALU.add)
                own(ins)
                return ins

            def tokens(kind, what, i, hh, g):
                dve.wait_ge(w_used, ends[what, i, hh, g])
                pair = {"q": 0, "k": 2, "kv": 2, "v": 6}[what]
                if what in ("q", "k", "kv"):
                    for t in range(NT):
                        if kind == "sb":
                            if what == "q":
                                ins = dve.tensor_scalar(qk[:, t, :], ps[:, pair + t, :], HD ** -0.5, None, ALU.mult)
                            else:
                                ins = dve.tensor_copy(qk[:, t, :], ps[:, pair + t, :])
                        elif what == "kv":
                            d = qk[:, t, 0:256].rearrange("p (h w d) -> p h w d", h=2, w=2)
                            rotate([d[:, :, 0, :], d[:, :, 1, :]], pair + t, 2, ("ck", "sk", "nsk"), t)
                        else:
                            rotate([qk[:, t, :].rearrange("p (h d) -> p h d", d=HD)], pair + t, 8,
                                   ("cq", "sq", "nsq") if what == "q" else ("ck", "sk", "nsk"), t)
                    if kind == "sb":
                        ins.then_inc(tok_done.sem, 1)
                    else:
                        dve.sem_inc(tok_done.sem, 1)
                if what == "v":
                    ins = dve.tensor_copy(vv[:, g, :, :], ps[:, pair:pair + 2, :])
                    ins.then_inc(v_done.sem, 1)
                if what == "kv":
                    ins = dve.tensor_copy(vv[:, 0, :, 0:P], ps[:, pair:pair + 2, P:2 * P])
                    ins.then_inc(v_done.sem, 1)

            def softmax_half(kind, i, hh):
                ng = NG if kind == "dil" else 1

                def scores(h, t):
                    n = 2 * h + t
                    wait(dve, acc_ready, "z", i, hh, h, t)
                    w = (t + 1) * ng * P
                    if n >= 2:
                        wait(dve, t_ready, "e", i, hh, h - 1, t)
                    bank = h % 2 if t == 0 else 2
                    z = ps[:, bank:bank + 2, :].rearrange("p b n -> p (b n)")[:, 0:w] if t else ps[:, bank, 0:w]
                    table = const(kind)
                    m = table[:, 0:ng * P] if t == 0 else table[:, ng * P:3 * ng * P]
                    c = t * 8 + h
                    low = const("sink")[:, hh * 8 + h:hh * 8 + h + 1] if kind == "swa" else NEG
                    own(dve.tensor_tensor_reduce(sc[:, n % 2, 0:w], z, m, 1.0, low, ALU.add, ALU.max, nmx[:, 0, c:c + 1]))
                    dve.tensor_scalar(nmx[:, 1, c:c + 1], nmx[:, 0, c:c + 1], -1.0, None, ALU.mult).then_inc(s_done.sem, 1)

                def evac1(h):
                    wait(dve, t_ready, "e", i, hh, h, 1)
                    n = 2 * ng
                    dve.tensor_copy(eT[:, 1, 0:n, :].rearrange("p c m -> p (c m)"),
                                    ps[:, 6:8, :].rearrange("p b n -> p (b n)")[:, 0:n * P]).then_inc(eT1_done.sem, 1)
                scores(0, 0)
                scores(0, 1)
                for h in range(HALF):
                    if h + 1 < HALF:
                        scores(h + 1, 0)
                    evac1(h)
                    if h + 1 < HALF:
                        scores(h + 1, 1)
                if kind == "swa":
                    wait(dve, sk_done, i, hh)
                    own(dve.tensor_tensor(nmx[:, 2, :], nmx[:, 2, :], nmx[:, 0, :], ALU.add))
                wait(dve, acc_ready, "o", i, hh)
                own(dve.reciprocal(nmx[:, 0, :], nmx[:, 2, :]))
                for t in range(NT):
                    r = nmx[:, 0, t * 8:(t + 1) * 8].unsqueeze(2).broadcast_to((P, 8, HD))
                    ins = dve.tensor_tensor(o[:, t, hh * BLK:(hh + 1) * BLK].rearrange("p (h d) -> p h d", d=HD),
                                            ps[:, 4 + t, :].rearrange("p (h d) -> p h d", d=HD), r, ALU.mult)
                ins.then_inc(o_done.sem, 1)

            def stick_half(i, hh):
                def tri(v):
                    return v.rearrange("p (m q) -> p m q", m=3)[:, 0:3:2, :]

                def soft(h):
                    wait(dve, ln_done, "l", i, hh, h)
                    s = ssp[:, h % 2, :]
                    own(dve.scalar_tensor_tensor(s, ps[:, h % 4, 0:384], 0.0, sw[:, h % 2, 0:384], ALU.max, ALU.add))
                    dve.tensor_tensor(tri(s), tri(s), const("keep").unsqueeze(1).broadcast_to((P, 2, P)),
                                      ALU.mult).then_inc(sp_done.sem, 1)

                def diag(h):
                    wait(dve, cum_done, "c", i, hh, h)
                    dve.tensor_tensor(tri(sa[:, h % 2, :]), tri(ps[:, h % 4, 0:384]),
                                      const("kill").unsqueeze(1).broadcast_to((P, 2, P)), ALU.add).then_inc(dm_done.sem, 1)
                soft(0)
                for h in range(HALF):
                    diag(h)
                    if h + 1 < HALF:
                        soft(h + 1)
                wait(dve, acc_ready, "o", i, hh)
                dve.tensor_copy(o[:, :, hh * BLK:(hh + 1) * BLK], ps[:, 4:6, :]).then_inc(o_done.sem, 1)

            def mix(l, i):
                kind = mixer_of(l)
                todo = None
                for what, hh, g in triples_of(l):
                    if what == "attn":
                        if todo:
                            tokens(*todo)
                            todo = None
                        stick_half(i, hh) if kind == "sb" else softmax_half(kind, i, hh)
                        continue
                    nu = units_of(what)
                    split(nu)
                    tokens(kind, what, i, hh, g)
                stream_t("o", i, 0)
                stream_t("o", i, 1)
                split(4)

            def ple(i):
                split(2)
                wait(dve, th_done, "p", i)
                dve.tensor_tensor(ptl[:], ps[:, 0, :].rearrange("p (c t m) -> p c t m", c=2, t=NT), pth[:].bitcast(F32),
                                  ALU.subtract).then_inc(tl_done.sem, 1)
                split(4)

            dve.wait_ge(c_landed, 16)
            dve.wait_ge(p_landed, 16)
            split(LEAD)
            for t in range(NT):
                stream_t("x", 0, t)
            for kind, l, i, u0, n in stages:
                assert st["u"] == u0 + LEAD, (kind, st["u"], u0)
                if kind in ("ffn1", "ffn2"):
                    ffn(i)
                elif kind == "mix":
                    mix(l, i)
                else:
                    ple(i)
                split(2)
                boundary(kind, i)

        @block.tensor
        def _(pe):
            st = {"u": 0}

            def three(out_, a_h, a_l, u, k, ncol, start, stop, cols=None):
                b_h = view(wh, u % RING, ncol)[:, k, :]
                b_l = view(wl, u % RING, ncol)[:, k, :]
                pe.matmul(out_, a_h, b_h, start=start, stop=False)
                pe.matmul(out_, a_h, b_l, start=False, stop=False)
                return pe.matmul(out_, a_l, b_h, start=False, stop=stop)

            def unit(u, t, bank, chunk0, ncol, ah, al, start, stop):
                nk = UW // ncol
                for k in range(nk):
                    ins = three(ps[:, bank, 0:ncol], ah[:, chunk0 + k, t, :], al[:, chunk0 + k, t, :], u, k, ncol,
                                start and k == 0, stop and k == nk - 1)
                return ins

            def ready(u, du=0):
                pe.wait_ge(lo_done, u + 1 + du)

            def run(items, by_tile, between=None, du=0, y=False):
                u = st["u"]
                st["u"] += len(items)
                if by_tile:
                    for t in range(NT):
                        if t and between:
                            between()
                        for n, it in enumerate(items):
                            if t == 0:
                                ready(u + n, du)
                            ins = unit(u + n, t, *it(t))
                            if t == NT - 1:
                                ins.then_inc(w_used, 1)
                        if t == 0 and y:
                            ins.then_inc(acc_ready.sem, 1)
                else:
                    for n, it in enumerate(items):
                        ready(u + n, du)
                        for t in range(NT):
                            ins = unit(u + n, t, *it(t))
                        ins.then_inc(w_used, 1)

            def transposes(src, n, bank, t, at=0):
                for c in range(n):
                    ins = pe.transpose(ps[:, bank + c // 4, (c % 4) * P:(c % 4 + 1) * P], src[:, at + c * P:at + (c + 1) * P], ident)
                return ins

            def stream_t(key, i, t):
                if key == "x" and i:
                    wait(pe, x_new, i - 1, t)
                elif key == "x":
                    pe.wait_ge(x_landed, 16)
                else:
                    wait(pe, o_done, i, 1)
                transposes((o if key == "o" else x)[:, t, :], 8, 2 * t, t).then_inc(t_ready.sem, 1)

            def y_items(nunits, ah, al, banks=lambda t, c: 4 + 2 * t + c, n0=0, chunk0=0, first=True, last=True):
                items = []
                for n in range(nunits):
                    k, c = n // 2, n % 2
                    items.append(lambda t, k=k, c=c: (banks(t, c), chunk0 + 2 * k, BLK, ah, al, first and k == 0,
                                                      last and k == nunits // 2 - 1))
                return items

            def col_items(pair, ncol, ah=xh, al=xl):
                nk = UW // ncol
                n = 8 // nk
                return [lambda t, m=m: (pair + t, m * nk, ncol, ah, al, m == 0, m == n - 1) for m in range(n)]

            def hidden_t(i, j, n, dj=0):
                pe.wait_ge(h_done.sem, h_done.at(i, j) + dj)
                for t in range(NT):
                    ins = transposes(hb[:, t, :], n, 2 + t, t)
                ins.then_inc(t_ready.sem, 1)

            def begin(i, between_key="x"):
                stream_t("x", i, 0)
                wait(pe, tl_done, "x", i, 0)

            def second(i, key="x"):
                def f():
                    stream_t(key, i, 1)
                    wait(pe, tl_done, key, i, 1)
                return f

            def ffn(i):
                begin(i)
                run(col_items(0, BLK), True, second(i))
                run(col_items(2, BLK), False)
                def block_of(j, dj, first):
                    du = 12 * dj
                    g = col_items(0, BLK)
                    pe.wait_ge(silu_done.sem, silu_done.at(i, j - 1) + dj)
                    run(g[0:3], False, du=du)
                    hidden_t(i, j - 1, 4, dj)
                    run(g[3:4], False, du=du)
                    pe.wait_ge(tl_done.sem, tl_done.at("h", i, j - 1) + dj)
                    run(y_items(4, hth, htl, first=first, last=False), False, du=du)
                    run(col_items(2, BLK), False, du=du)

                block_of(1, 0, True)
                with pe.Fori(0, NJ - 2) as r:
                    block_of(2, r, False)
                st["u"] += 12 * (NJ - 3)
                g = col_items(0, 256)
                wait(pe, silu_done, i, NJ - 1)
                run(g[0:1], False)
                hidden_t(i, NJ - 1, 4)
                run(g[1:2], False)
                wait(pe, tl_done, "h", i, NJ - 1)
                run(col_items(2, 256), False)
                down = y_items(4, hth, htl, first=False, last=False)
                run(down[0:2], False)
                hidden_t(i, NJ, 2)
                last = y_items(2, hth, htl, chunk0=4, first=False)
                items = down[2:4] + [lambda t, f=last[0]: (wait(pe, tl_done, "h", i, NJ), f(t))[1], last[1]]
                run(items, True, y=True)

            def attn_z(i, hh, h, t, ng, kc):
                pb = HD * (h % 2)
                for g in range(ng):
                    for kb in range(t + 1):
                        w = g * (t + 1) + kb
                        bank = h % 2 if t == 0 else 2 + w // 4
                    bank = h % 2 if t == 0 else 2 + (g * 256) // BLK
                    at = (g * (t + 1) * P) % BLK
                    ins = pe.matmul(ps[:, bank, at:at + (t + 1) * P], qT[pb:pb + HD, g, h // 2, t * P:(t + 1) * P],
                                    kT[pb:pb + HD, g, h // 2 if kc is None else kc, 0:(t + 1) * P], start=True, stop=True)
                ins.then_inc(acc_ready.sem, 1)

            def softmax_half(kind, i, hh):
                ng = NG if kind == "dil" else 1
                kc = None if kind == "dil" else hh
                order = [(h, t) for h in range(HALF) for t in range(NT)]

                def z(n):
                    h, t = order[n]
                    if t == 0 and h >= 2:
                        wait(pe, s_done, i, hh, h - 2, 0)
                    if t == 1 and h >= 1:
                        wait(pe, s_done, i, hh, h - 1, 1)
                    attn_z(i, hh, h, t, ng, kc)

                def tr(n):
                    h, t = order[n]
                    wait(pe, e_done, i, hh, h, t)
                    transposes(sc[:, n % 2, :], ng * (t + 1), 6, t).then_inc(t_ready.sem, 1)

                def av(n):
                    h, t = order[n]
                    wait(pe, (eT0_done, eT1_done)[t], i, hh, h)
                    m = 0
                    for g in range(ng):
                        for kb in range(t + 1):
                            v = vv[:, g, kb, h * HD:(h + 1) * HD] if kind == "dil" else vv[:, 0, kb, hh * HD:(hh + 1) * HD]
                            ins = pe.matmul(ps[:, 4 + t, h * HD:(h + 1) * HD], eT[:, t, m, :], v,
                                            start=m == 0, stop=m == ng * (t + 1) - 1)
                            m += 1
                    return ins
                z(0)
                for n in range(len(order)):
                    if n + 1 < len(order):
                        z(n + 1)
                    if n:
                        av(n - 1)
                    tr(n)
                av(len(order) - 1).then_inc(acc_ready.sem, 1)

            def stick_half(i, hh):
                def z(h):
                    pb = HD * (h % 2)
                    pe.matmul(ps[:, h % 4, 0:S], kT[pb:pb + HD, 0, h // 2, 0:P], qT[pb:pb + HD, 0, h // 2, :], start=True, stop=False)
                    pe.matmul(ps[:, h % 4, S:S + P], kT[pb:pb + HD, 0, h // 2, P:S], qT[pb:pb + HD, 0, h // 2, P:S],
                              start=False, stop=True).then_inc(acc_ready.sem, 1)

                def cum(h):
                    wait(pe, sp_done, "s", i, hh, h)
                    pe.matmul(ps[:, h % 4, 0:384], const("lower"), ssp[:, h % 2, :], start=False, stop=False, skip_group_check=True)
                    pe.matmul(ps[:, h % 4, P:2 * P], const("ones"), ssp[:, h % 2, 2 * P:3 * P], start=False, stop=True,
                              skip_group_check=True).then_inc(cum_done.sem, 1)

                def av(h):
                    wait(pe, a_done, "a", i, hh, h)
                    a = sa[:, h % 2, :]
                    c = slice(h * HD, (h + 1) * HD)
                    pe.matmul(ps[:, 4, c], a[:, 0:P], vv[:, 0, 0, c], start=True, stop=True)
                    pe.matmul(ps[:, 5, c], a[:, P:2 * P], vv[:, 0, 0, c], start=True, stop=False)
                    return pe.matmul(ps[:, 5, c], a[:, 2 * P:3 * P], vv[:, 0, 1, c], start=False, stop=True)
                z(0)
                z(1)
                for h in range(HALF):
                    if h + 2 < HALF:
                        z(h + 2)
                    cum(h)
                    if h:
                        av(h - 1)
                av(HALF - 1).then_inc(acc_ready.sem, 1)

            def mix(l, i):
                kind = mixer_of(l)
                begin(i)
                pending = None
                steps = triples_of(l)

                def head_t(what, hh, g):
                    wait(pe, tok_done, what, i, hh, g)
                    for t in range(NT):
                        ins = transposes(qk[:, t, :], 2 if what == "kv" else 4, 4 + t, t)
                    ins.then_inc(t_ready.sem, 1)
                first = True
                used = {}
                copied = None
                for what, hh, g in steps:
                    if what == "attn":
                        if pending:
                            if copied:
                                wait(pe, th_done, *copied)
                            head_t(*pending)
                            copied = (pending[0], i, pending[1], pending[2])
                            pending = None
                        wait(pe, th_done, *copied)
                        wait(pe, v_done, i, 0 if kind == "swa" else hh, NG - 1 if kind == "dil" else 0)
                        stick_half(i, hh) if kind == "sb" else softmax_half(kind, i, hh)
                        if hh == 0:
                            wait(pe, o_done, i, 0)
                        used = {}
                        continue
                    pair = {"q": 0, "k": 2, "kv": 2, "v": 6}[what]
                    if pair in used:
                        if pair == 6:
                            wait(pe, v_done, *used[pair])
                        else:
                            wait(pe, tok_done, *used[pair])
                    used[pair] = (i, hh, g) if what == "v" else (what, i, hh, g)
                    items = col_items(pair, 256 if what == "kv" else BLK)
                    if first:
                        run(items, True, second(i))
                        first = False
                    else:
                        run(items[:-1], False)
                        if pending:
                            if copied:
                                wait(pe, th_done, *copied)
                            head_t(*pending)
                            copied = (pending[0], i, pending[1], pending[2])
                            pending = None
                        run(items[-1:], False)
                    if what != "v":
                        pending = (what, hh, g)
                stream_t("o", i, 0)
                wait(pe, tl_done, "o", i, 0)
                y = y_items(8, xh, xl)
                run(y[0:4], True, second(i, "o"))
                run(y[4:8], True, y=True)

            def ple(l, i):
                begin(i)
                y = y_items(8, xh, xl)
                run(y[0:4], True, second(i))
                pe.wait_ge(p_landed, 16 * (l + 2))
                for t in range(NT):
                    for c in range(2):
                        ins = pe.transpose(ps[:, 0, (2 * c + t) * P:(2 * c + t + 1) * P], pin[:, t, c * P:(c + 1) * P], ident)
                ins.then_inc(t_ready.sem, 1)
                run(y[4:6], False)
                pr = y_items(2, pth, ptl, banks=lambda t, c: 2 * t + c)

                run(y[6:8], False)
                wait(pe, tl_done, "p", i)
                run(pr, True, y=True)

            pe.wait_ge(c_landed, 16)
            for kind, l, i, u0, n in stages:
                assert st["u"] == u0, (kind, st["u"], u0)
                if kind in ("ffn1", "ffn2"):
                    ffn_done = ffn(i)
                elif kind == "mix":
                    mix(l, i)
                else:
                    ple(l, i)


def constants():
    import numpy as np
    t = np.zeros((P, CONST["sink"][0]), np.float32)

    def put(name, v):
        a, b = CONST[name]
        t[:, a:b] = v
    p, q = np.arange(P)[:, None], np.arange(P)[None, :]
    put("ident", p == q)
    put("lower", -1.0 * (p >= q))
    put("ones", -1.0)
    put("keep", p < q)
    put("kill", np.where(p < q, 0.0, NEG))
    key = np.arange(S)[None, :]

    def banded(ok):
        return [np.where(ok(t * P + p - key[:, 0:(t + 1) * P]), 0.0, NEG) for t in range(NT)]
    put("swa", np.concatenate(banded(lambda d: (d >= 0) & (d <= 127)), 1))
    per = [banded(lambda d, w=w, s=s: (d >= 0) & (d % s == 0) & (d // s <= w // s)) for w, s in DIL]
    put("dil", np.concatenate([m[t] for t in range(NT) for m in per], 1))
    pos = np.arange(S, dtype=np.float32)
    inv = np.float32(10000.0) ** (-np.arange(0, HD, 2, dtype=np.float32) / np.float32(HD))
    ang = (pos[:, None] * inv[None, :]).astype(np.float32)
    c, s = np.cos(ang), np.sin(ang)
    rows = lambda m: np.concatenate([m[0:P], m[P:S]], 1)
    for name, m in (("cq", c * HD ** -0.5), ("sq", s * HD ** -0.5), ("nsq", -s * HD ** -0.5), ("ck", c), ("sk", s), ("nsk", -s)):
        put(name, rows(m))
    return t


_INS = ['x', 'p', 'ffn1_w_in', 'ffn1_w_out', 'ffn2_w_in', 'ffn2_w_out', 'ln_g', 'ln_b', 'sb_w_in', 'sb_w_out',
        'swa_w_in', 'swa_sinks', 'swa_w_out', 'dil_w_in', 'dil_w_out', 'ple_w_proj', 'ple_w_gate']


def kernel(**inputs):
    import numpy as np
    import concourse.bacc as bacc
    from concourse.bass_utils import run_bass_kernel_spmd

    nc = bacc.Bacc("TRN2", target_bir_lowering=False, num_devices=1)
    arrays, aps = {}, {}
    for name in _INS:
        arrays[f"in_{name}"] = np.ascontiguousarray(inputs[name])
    arrays["in_consts"] = constants()
    for name in _INS + ["consts"]:
        a = arrays[f"in_{name}"]
        aps[name] = nc.dram_tensor(f"in_{name}", a.shape, mybir.dt.from_np(a.dtype), kind="ExternalInput").ap()
    out = nc.dram_tensor("out_dram", (1, S, D), F32, kind="ExternalOutput").ap()
    build_program(nc, aps, out)
    r = run_bass_kernel_spmd(nc, [arrays], core_ids=[0])
    return r.results[0]["out_dram"]
```

```python
from contextlib import ExitStack

import concourse.bass as bass
from concourse import mybir

F32 = mybir.dt.float32
F32R = mybir.dt.float32r
I32 = mybir.dt.int32
ALU = mybir.AluOpType
ACT = mybir.ActivationFunctionType

P = 128
D = 1024
S = 256
NT = S // P
DEPTH = 4
FF = 2816
PLE = 256
HD = 64
HALF = 8
PAIRS = HALF // 2
ALPHA = (2 * DEPTH) ** 0.25
EPS = 1e-5
NEG = -1e30
RING = 6
LEAD = 4
UW = 1024
BLK = 512
NJ = FF // BLK
DIL = ((128, 1), (512, 4), (2048, 16))
NG = len(DIL)

CONST = {}
_at = 0
for _name, _n in (("ident", P), ("lower", P), ("ones", P), ("keep", P), ("kill", P), ("swa", 3 * P),
                  ("dil", 3 * NG * P), ("cq", 64), ("sq", 64), ("nsq", 64), ("ck", 64), ("sk", 64), ("nsk", 64),
                  ("sink", 16)):
    CONST[_name] = (_at, _at + _n)
    _at += _n
CONST_W = _at


def mixer_of(l):
    return ("sb", "swa", "dil")[l % 3]


class Signal:

    def __init__(self, sem):
        self.sem, self.place = sem, {}

    def note(self, *key):
        self.place[key] = len(self.place) + 1

    def at(self, *key):
        return self.place[key]


def triples_of(l):
    kind = mixer_of(l)
    if kind == "swa":
        return [("q", 0, 0), ("kv", 0, 0), ("attn", 0, 0), ("q", 1, 0), ("attn", 1, 0)]
    steps = []
    for hh in range(2):
        for g in range(NG if kind == "dil" else 1):
            steps += [("q", hh, g), ("k", hh, g), ("v", hh, g)]
        steps.append(("attn", hh, 0))
    return steps


def units_of(step):
    return 2 if step == "kv" else 4


def build_program(nc, A, out):
    ctx = ExitStack()
    with ctx:
        def sb(name, shape, dt=F32):
            return ctx.enter_context(nc.sbuf_tensor(name, shape, dt))

        raw = sb("raw", [P, RING, UW])
        wh = sb("wh", [P, RING, UW], F32R)
        wl = sb("wl", [P, RING, UW], F32R)
        x = sb("x", [P, NT, D])
        xh = sb("xh", [P, D // P, NT, P], F32R)
        xl = sb("xl", [P, D // P, NT, P], F32R)
        hth = sb("hth", [P, 6, NT, P], F32R)
        htl = sb("htl", [P, 6, NT, P], F32R)
        pth = sb("pth", [P, 2, NT, P], F32R)
        ptl = sb("ptl", [P, 2, NT, P], F32R)
        pin = sb("pin", [P, NT, PLE])
        gb = sb("gb", [P, 2, D])
        consts = sb("consts", [P, CONST_W])
        rsum = sb("rsum", [P, NT, 2])
        nmean = sb("nmean", [P, NT, 1])
        ssq = sb("ssq", [P, NT, 1])
        veps = sb("veps", [P, NT, 1])
        rstd = sb("rstd", [P, NT, 1])
        mhalf = sb("mhalf", [P, 1])
        nmx = sb("nmx", [P, 5, 16])
        arena = sb("arena", [P, 15360])
        place = [0]

        def part(n):
            place[0] += n
            return arena[:, place[0] - n:place[0]]

        qT = part(NG * 4 * S).rearrange("p (g c s) -> p g c s", g=NG, c=4)
        kT = part(NG * 4 * S).rearrange("p (g c s) -> p g c s", g=NG, c=4)
        vv = part(NG * NT * BLK).rearrange("p (g t n) -> p g t n", g=NG, t=NT)
        qk = part(NT * BLK).rearrange("p (t n) -> p t n", t=NT)
        ra = part(BLK)
        rb = part(BLK)
        sc = part(2 * 768).rearrange("p (b n) -> p b n", b=2)
        eT = part(2 * 768).rearrange("p (b m q) -> p b m q", b=2, m=6)
        o = part(4 * S).rearrange("p (c t m) -> p c t m", c=4, t=NT)
        sg = arena[:, 0:NT * BLK].rearrange("p (t n) -> p t n", t=NT)
        hb = arena[:, NT * BLK:2 * NT * BLK].rearrange("p (t n) -> p t n", t=NT)
        eg = arena[:, 0:NT * D].rearrange("p (t n) -> p t n", t=NT)
        xn = arena[:, 0:NT * D].rearrange("p (t n) -> p t n", t=NT)
        sq = arena[:, NT * D:NT * D + D]
        def pair_buffer(of):
            v = of[:, 1:3].rearrange("p g c s -> p (g c s)")[:, 0:4 * 384]
            return v.rearrange("p (b h n) -> p b h n", b=2, h=2)
        sw = pair_buffer(qT)
        ssp = pair_buffer(kT)
        sa = pair_buffer(vv)

        ps = ctx.enter_context(nc.psum_tensor("ps", [P, 8, BLK], F32))

        def zpair(h):
            b = (4, 6)[h % 2]
            return ps[:, b:b + 2, 0:384]

        def opair(h):
            return ps[:, 2 + h // 4, (h // 2) % 2 * S:((h // 2) % 2 + 1) * S]

        oall = ps[:, 2:4, :].rearrange("p b (c t m) -> p (b c) t m", c=2, t=NT)

        def diagonals(v):
            return v.rearrange("p h (m q) -> p h m q", q=P)[:, :, 0:3:2, :]

        def const(name):
            a, b = CONST[name]
            return consts[:, a:b]

        ident = const("ident")

        def signal(name):
            return Signal(ctx.enter_context(nc.semaphore(name)))

        def semaphore(name):
            return ctx.enter_context(nc.semaphore(name))

        landed = [semaphore(f"landed{s}") for s in range(RING)]
        hi_done = semaphore("hi_done")
        lo_done = semaphore("lo_done")
        w_used = semaphore("w_used")
        x_landed = semaphore("x_landed")
        c_landed = semaphore("c_landed")
        g_landed = semaphore("g_landed")
        b_landed = semaphore("b_landed")
        p_landed = semaphore("p_landed")
        stored = [semaphore(f"stored{t}") for t in range(NT)]
        acc_ready = signal("acc_ready")
        t_ready = signal("t_ready")
        th_done = signal("th_done")
        tl_done = signal("tl_done")
        silu_done = signal("silu_done")
        h_done = signal("h_done")
        x_new = signal("x_new")
        mean_done = signal("mean_done")
        ssq_done = signal("ssq_done")
        rstd_done = signal("rstd_done")
        tok_done = signal("tok_done")
        v_done = signal("v_done")
        s_done = signal("s_done")
        e_done = signal("e_done")
        eT0_done = signal("eT0_done")
        eT1_done = signal("eT1_done")
        p_done = signal("p_done")
        ln_done = signal("ln_done")
        sp_done = signal("sp_done")
        cum_done = signal("cum_done")
        dm_done = signal("dm_done")
        a_done = signal("a_done")
        o_done = signal("o_done")
        sig_done = signal("sig_done")
        own_act = semaphore("own_act")
        own_dve = semaphore("own_dve")
        mh_done = semaphore("mh_done")

        stages = []
        u = 0
        for l in range(DEPTH):
            for kind in ("ffn1", "mix", "ffn2", "ple"):
                n = {"ffn1": 66, "ffn2": 66, "ple": 10, "mix": 8 + sum(units_of(s[0]) for s in triples_of(l) if s[0] != "attn")}[kind]
                stages.append((kind, l, len(stages), u, n))
                u += n
        UNITS = u
        NST = len(stages)

        ends = {}
        def note_stream(key, i):
            for t in range(NT):
                for c in range(2):
                    t_ready.note(key, i, t, c), th_done.note(key, i, t, c), tl_done.note(key, i, t, c)

        note_stream("x", 0)
        for kind, l, i, u0, n in stages:
            if kind in ("ffn1", "ffn2"):
                for j in range(NJ + 1):
                    base = u0 if j == 0 else u0 + 8 + 12 * (j - 1)
                    ends["gate", i, j] = base + (4 if j < NJ else 2)
                    ends["up", i, j] = base + (8 if j == 0 else 12 if j < NJ else 4)
                    silu_done.note(i, j), h_done.note(i, j)
                    t_ready.note("h", i, j), th_done.note("h", i, j), tl_done.note("h", i, j)
            elif kind == "mix":
                at = u0
                for what, hh, g in triples_of(l):
                    if what != "attn":
                        at += units_of(what)
                        ends[what, i, hh, g] = at
                        if what != "v":
                            tok_done.note(what, i, hh, g)
                            t_ready.note(what, i, hh, g), th_done.note(what, i, hh, g)
                        if what in ("v", "kv"):
                            v_done.note(i, hh, g)
                    elif mixer_of(l) == "sb":
                        for h in range(PAIRS):
                            for one in (ln_done, sp_done, cum_done, dm_done, a_done):
                                one.note(i, hh, h)
                            acc_ready.note("z", i, hh, h)
                        acc_ready.note("o", i, hh)
                    else:
                        for h in range(HALF):
                            for t in range(NT):
                                acc_ready.note("z", i, hh, h, t), s_done.note(i, hh, h, t), e_done.note(i, hh, h, t)
                                t_ready.note("e", i, hh, h, t)
                                (eT0_done, eT1_done)[t].note(i, hh, h)
                                p_done.note(i, hh, h, t)
                        acc_ready.note("o", i, hh)
                o_done.note(i)
                for c in range(2):
                    th_done.note("o", i, c), tl_done.note("o", i, c)
            else:
                ends["gate", i] = u0 + 8
                t_ready.note("p", i), th_done.note("p", i), tl_done.note("p", i), sig_done.note(i)
            ends["y", i] = u0 + n
            acc_ready.note("y", i, 0), acc_ready.note("y", i, 1)
            for t in range(NT):
                x_new.note(i, t, 0), x_new.note(i, t, 1)
                if kind != "ple":
                    mean_done.note(i, t), ssq_done.note(i, t), rstd_done.note(i, t)
            if i + 1 < NST:
                note_stream("x", i + 1)

        norm_index = {i: 3 * l + ("ffn1", "mix", "ffn2").index(kind) for kind, l, i, _, _ in stages if kind != "ple"}

        def wait(eng, sig, *key):
            eng.wait_ge(sig.sem, sig.at(*key))

        def view(ring, slot, ncol):
            return ring[:, slot, :].rearrange("p (k n) -> p k n", n=ncol)

        block = ctx.enter_context(nc.Block())

        @block.sync
        def _(sp):
            st = {"u": 0}

            def load(src, rows, cols, ncol, base=None):
                u = st["u"]
                st["u"] += 1
                if u >= RING:
                    sp.wait_ge(lo_done, u - RING + 1 + (0 if base is None else base))
                nk = UW // ncol
                v = src.rearrange("(k p) n -> p k n", p=P)
                sp.dma_start(view(raw, u % RING, ncol),
                             v[:, bass.ds(rows, nk), bass.ds(cols, ncol)]).then_inc(landed[u % RING], 16)

            def ffn(l, i, win, wout):
                def block_of(j, base, first=False):
                    for k in range(0, 8, 2):
                        load(win, k, j * BLK, BLK, base)
                    if not first:
                        for k in range(2):
                            for c in range(2):
                                load(wout, j * 4 - 4 + 2 * k, c * BLK, BLK, base)
                    for k in range(0, 8, 2):
                        load(win, k, j * BLK + FF, BLK, base)
                block_of(0, None, True)
                norm_load(i)
                with sp.Fori(0, NJ - 1) as r:
                    block_of(r + 1, r * 12)
                st["u"] += 12 * (NJ - 2)
                for c in (NJ * BLK, NJ * BLK + FF):
                    for k in (0, 4):
                        load(win, k, c, 256)
                down = [(NJ * 4 - 4 + 2 * k, c) for k in range(3) for c in range(2)]
                for k, c in down[0:2] + sorted(down[2:6], key=lambda kc: kc[1]):
                    load(wout, k, c * BLK, BLK)

            def norm_load(i):
                n = norm_index[i]
                if n:
                    before = i - 1 if i - 1 in norm_index else i - 2
                    wait(sp, x_new, before, 1, 1)
                sp.dma_start(gb[:, 0, :], A["ln_g"].rearrange("l k n -> (l k) n")[n].partition_broadcast(P)).then_inc(g_landed, 16)
                sp.dma_start(gb[:, 1, :], A["ln_b"].rearrange("l k n -> (l k) n")[n].partition_broadcast(P)).then_inc(b_landed, 16)

            sp.dma_start(x[:], A["x"][0].rearrange("(t p) n -> p t n", p=P)).then_inc(x_landed, 16)
            sp.dma_start(consts[:, 0:CONST["sink"][0]], A["consts"]).then_inc(c_landed, 16)
            sp.dma_start(const("sink"), A["swa_sinks"][0].partition_broadcast(P)).then_inc(p_landed, 16)
            for kind, l, i, u0, n in stages:
                assert st["u"] == u0, (kind, st["u"], u0)
                if kind == "ffn1":
                    ffn(l, i, A["ffn1_w_in"][l], A["ffn1_w_out"][l])
                elif kind == "ffn2":
                    ffn(l, i, A["ffn2_w_in"][l], A["ffn2_w_out"][l])
                elif kind == "mix":
                    name = mixer_of(l)
                    win, wout = A[f"{name}_w_in"][l // 3], A[f"{name}_w_out"][l // 3]
                    for n, (what, hh, g) in enumerate(triples_of(l)):
                        if n == 2:
                            norm_load(i)
                        if what == "kv":
                            for k in (0, 4):
                                load(win, k, D, 256)
                        elif what != "attn":
                            col = g * 3 * D + "qkv".index(what) * D + hh * BLK
                            for k in range(0, 8, 2):
                                load(win, k, col, BLK)
                    y = [(k, c) for k in range(0, 8, 2) for c in range(2)]
                    for k, c in y[0:4] + sorted(y[4:8], key=lambda kc: kc[1]):
                        load(wout, k, c * BLK, BLK)
                else:
                    if l:
                        wait(sp, t_ready, "p", i - 4)
                    sp.dma_start(pin[:], A["p"][l, 0].rearrange("(t p) n -> p t n", p=P)).then_inc(p_landed, 16)
                    for k in range(0, 8, 2):
                        for c in range(2):
                            load(A["ple_w_gate"][l], k, c * BLK, BLK)
                    for c in range(2):
                        load(A["ple_w_proj"][l], 0, c * BLK, BLK)
            for t in range(NT):
                wait(sp, x_new, NST - 1, t, 1)
                sp.dma_start(out[0].rearrange("(t p) n -> p t n", p=P)[:, t, :], x[:, t, :]).then_inc(stored[t], 16)
            for t in range(NT):
                sp.wait_ge(stored[t], 16)

        @block.gpsimd
        def _(pool):
            pool.memset(mhalf[:], -0.5).then_inc(mh_done, 1)
            pool.wait_ge(mh_done, 1)
            for kind, l, i, u0, n in stages:
                if kind != "ple":
                    for t in range(NT):
                        wait(pool, ssq_done, i, t)
                        pool.tensor_scalar(veps[:, t, :], ssq[:, t, :], 1.0 / D, EPS, ALU.mult, ALU.add).then_inc(mh_done, 1)
                        pool.wait_ge(mh_done, 2 + 2 * norm_index[i] + t)
                        pool.tensor_tensor(rstd[:, t, :], veps[:, t, :], mhalf[:], ALU.pow).then_inc(rstd_done.sem, 1)

        @block.scalar
        def _(act):
            st = {"u": 0, "own": 0}

            def own(ins):
                st["own"] += 1
                ins.then_inc(own_act, 1)
                act.wait_ge(own_act, st["own"])

            def split(n=1, loop=None):
                for _ in range(n):
                    u = st["u"]
                    if u >= UNITS:
                        return
                    st["u"] += 1
                    du, dr = loop or (0, 0)
                    act.wait_ge(landed[u % RING], 16 * (u // RING + 1) + dr)
                    if u >= RING:
                        act.wait_ge(w_used, u - RING + 1 + du)
                    act.activation(wh[:, u % RING, :], raw[:, u % RING, :], ACT.Copy).then_inc(hi_done, 1)

            def stream_t(key, i, t):
                for c in range(2):
                    wait(act, t_ready, key, i, t, c)
                    act.activation(xh[:, 4 * c:4 * c + 4, t, :], ps[:, 2 * t + c, :].rearrange("p (k m) -> p k m", m=P),
                                   ACT.Copy).then_inc(th_done.sem, 1)

            def hidden_t(i, j, n, at, dj=0):
                act.wait_ge(t_ready.sem, t_ready.at("h", i, j) + dj)
                for t in range(NT):
                    ins = act.activation(hth[:, at:at + n, t, :], ps[:, 2 + t, 0:n * P].rearrange("p (c m) -> p c m", m=P), ACT.Copy)
                ins.then_inc(th_done.sem, 1)

            def silu(i, j, n, dj=0):
                act.wait_ge(w_used, ends["gate", i, j] + 12 * dj)
                for t in range(NT):
                    ins = act.activation(sg[:, t, 0:n], ps[:, t, 0:n], ACT.Silu)
                ins.then_inc(silu_done.sem, 1)

            def ffn(i):
                split(8 - 4)
                silu(i, 0, BLK)
                split(4)
                with act.Fori(0, NJ - 1) as r:
                    lp = (r * 12, r * 32)
                    split(3, lp)
                    hidden_t(i, 0, 4, 0, r)
                    split(2, lp)
                    silu(i, 1, BLK, r)
                    split(7, lp)
                st["u"] += 12 * (NJ - 2)
                split(2)
                hidden_t(i, NJ - 1, 4, 0)
                silu(i, NJ, 256)
                split(4)
                hidden_t(i, NJ, 2, 4)

            def boundary(kind, i):
                for t in range(NT):
                    if kind != "ple":
                        wait(act, mean_done, i, t)
                        act.activation(sq, x[:, t, :], ACT.Square, bias=nmean[:, t, :], accum_out=ssq[:, t, :]).then_inc(ssq_done.sem, 1)
                    if i + 1 < NST:
                        if t == 0:
                            split(2)
                        stream_t("x", i + 1, t)

            def copy_t(what, i, hh, g, dst):
                wait(act, t_ready, what, i, hh, g)
                n = 2 if what == "kv" else 4
                for t in range(NT):
                    ins = act.activation(dst[:, g, 0:n, t * P:(t + 1) * P],
                                         ps[:, 4 + t, 0:n * P].rearrange("p (c m) -> p c m", m=P), ACT.Copy)
                ins.then_inc(th_done.sem, 1)

            def softmax_half(kind, i, hh):
                ng = NG if kind == "dil" else 1

                def exps(h, t):
                    n = 2 * h + t
                    wait(act, s_done, i, hh, h, t)
                    w = (t + 1) * ng * P
                    c = t * 8 + h
                    if kind == "swa":
                        act.activation(nmx[:, 3, c:c + 1], const("sink")[:, hh * 8 + h:hh * 8 + h + 1], ACT.Exp,
                                       bias=nmx[:, 1, c:c + 1])
                    act.activation(sc[:, n % 2, 0:w], sc[:, n % 2, 0:w], ACT.Exp, bias=nmx[:, 1, c:c + 1],
                                   accum_out=nmx[:, 2, c:c + 1]).then_inc(e_done.sem, 1)

                def evac0(h):
                    wait(act, t_ready, "e", i, hh, h, 0)
                    act.activation(eT[:, 0, 0:ng, :], ps[:, 6, 0:ng * P].rearrange("p (c m) -> p c m", m=P),
                                   ACT.Copy).then_inc(eT0_done.sem, 1)
                exps(0, 0)
                for h in range(HALF):
                    exps(h, 1)
                    evac0(h)
                    if h + 1 < HALF:
                        exps(h + 1, 0)

            def stick_half(i, hh):
                def logs(h):
                    wait(act, acc_ready, "z", i, hh, h)
                    if h >= 2:
                        wait(act, sp_done, i, hh, h - 2)
                    w = sw[:, h % 2]
                    own(act.activation(w, zpair(h), ACT.Abs))
                    own(act.activation(w, w, ACT.Exp, scale=-1.0))
                    act.activation(w, w, ACT.Ln, bias=1.0).then_inc(ln_done.sem, 1)

                def weights(h):
                    wait(act, dm_done, i, hh, h)
                    a = sa[:, h % 2]
                    act.activation(a[:, :, P:2 * P], zpair(h)[:, :, P:2 * P], ACT.Exp)
                    act.activation(diagonals(a), diagonals(a), ACT.Exp).then_inc(a_done.sem, 1)
                logs(0)
                logs(1)
                for h in range(PAIRS):
                    if hh == 0:
                        split(1)
                    weights(h)
                    if h + 2 < PAIRS:
                        logs(h + 2)

            def mix(l, i):
                kind = mixer_of(l)
                u_out = ends["y", i] - 8
                late = []
                for n, (what, hh, g) in enumerate(triples_of(l)):
                    if what == "attn":
                        for f in late:
                            f()
                        late = []
                        if hh == 1:
                            act.wait_ge(w_used, u_out)
                            act.activation(xh[:, 0:4], o, ACT.Copy).then_inc(th_done.sem, 1)
                        stick_half(i, hh) if kind == "sb" else softmax_half(kind, i, hh)
                        wait(act, acc_ready, "o", i, hh)
                        if hh == 0:
                            act.activation(o, oall, ACT.Copy).then_inc(o_done.sem, 1)
                        else:
                            act.activation(xh[:, 4:8], oall, ACT.Copy).then_inc(th_done.sem, 1)
                        continue
                    nu = units_of(what)
                    if kind == "sb" and (what, hh) == ("q", 1):
                        late = [lambda what=what, hh=hh, g=g: copy_t(what, i, hh, g, qT)]
                        continue
                    split(nu - 1)
                    for f in late:
                        f()
                    late = []
                    split(1)
                    if what != "v":
                        late = [lambda what=what, hh=hh, g=g: copy_t(what, i, hh, g, qT if what == "q" else kT)]
                split(4)

            def ple(i):
                split(2)
                wait(act, t_ready, "p", i)
                act.activation(pth[:], ps[:, 0, :].rearrange("p (c t m) -> p c t m", c=2, t=NT), ACT.Copy).then_inc(th_done.sem, 1)
                split(4)
                act.wait_ge(w_used, ends["gate", i])
                for t in range(NT):
                    ins = act.activation(eg[:, t, :], ps[:, 4 + 2 * t:6 + 2 * t, :].rearrange("p c n -> p (c n)"), ACT.Sigmoid)
                ins.then_inc(sig_done.sem, 1)

            split(LEAD)
            for t in range(NT):
                stream_t("x", 0, t)
            for kind, l, i, u0, n in stages:
                assert st["u"] == u0 + LEAD, (kind, st["u"], u0)
                if kind in ("ffn1", "ffn2"):
                    ffn(i)
                elif kind == "mix":
                    mix(l, i)
                else:
                    ple(i)
                split(2)
                boundary(kind, i)

        @block.vector
        def _(dve):
            st = {"u": 0, "own": 0}

            def own(ins):
                st["own"] += 1
                ins.then_inc(own_dve, 1)
                dve.wait_ge(own_dve, st["own"])

            def split(n=1, du=0):
                for _ in range(n):
                    u = st["u"]
                    if u >= UNITS:
                        return
                    st["u"] += 1
                    dve.wait_ge(hi_done, u + 1 + du)
                    dve.tensor_tensor(wl[:, u % RING, :], raw[:, u % RING, :], wh[:, u % RING, :].bitcast(F32),
                                      ALU.subtract).then_inc(lo_done, 1)

            def stream_t(key, i, t):
                for c in range(2):
                    wait(dve, th_done, key, i, t, c)
                    dve.tensor_tensor(xl[:, 4 * c:4 * c + 4, t, :], ps[:, 2 * t + c, :].rearrange("p (k m) -> p k m", m=P),
                                      xh[:, 4 * c:4 * c + 4, t, :].bitcast(F32), ALU.subtract).then_inc(tl_done.sem, 1)

            def hidden_t(i, j, n, at, dj=0):
                dve.wait_ge(th_done.sem, th_done.at("h", i, j) + dj)
                for t in range(NT):
                    ins = dve.tensor_tensor(htl[:, at:at + n, t, :], ps[:, 2 + t, 0:n * P].rearrange("p (c m) -> p c m", m=P),
                                            hth[:, at:at + n, t, :].bitcast(F32), ALU.subtract)
                ins.then_inc(tl_done.sem, 1)

            def hidden(i, j, n, dj=0):
                dve.wait_ge(silu_done.sem, silu_done.at(i, j) + dj)
                dve.wait_ge(w_used, ends["up", i, j] + 12 * dj)
                for t in range(NT):
                    ins = dve.scalar_tensor_tensor(hb[:, t, 0:n], sg[:, t, 0:n], 0.5, ps[:, 2 + t, 0:n], ALU.mult, ALU.mult)
                ins.then_inc(h_done.sem, 1)

            def ffn(i):
                split(8)
                hidden(i, 0, BLK)
                with dve.Fori(0, NJ - 1) as r:
                    split(3, r * 12)
                    hidden_t(i, 0, 4, 0, r)
                    split(9, r * 12)
                    hidden(i, 1, BLK, r)
                st["u"] += 12 * (NJ - 2)
                split(2)
                hidden_t(i, NJ - 1, 4, 0)
                split(2)
                hidden(i, NJ, 256)
                split(2)
                hidden_t(i, NJ, 2, 4)

            def y_wait(kind, i, t, c):
                if t == 0:
                    wait(dve, acc_ready, "y", i, c)
                else:
                    dve.wait_ge(w_used, ends["y", i] - (0 if c else 1 if kind == "ple" else 2))

            def residual(kind, i, t, c):
                y_wait(kind, i, t, c)
                h = slice(c * BLK, (c + 1) * BLK)
                return dve.scalar_tensor_tensor(x[:, t, h], x[:, t, h], ALPHA, ps[:, 4 + 2 * t + c, :], ALU.mult, ALU.add,
                                                accum_out=rsum[:, t, c:c + 1])

            def center(i, t, ins):
                own(ins)
                dve.tensor_scalar(nmean[:, t, :], rsum[:, t, 0:1], rsum[:, t, 1:2], -1.0 / D, ALU.add, ALU.mult).then_inc(mean_done.sem, 1)
                wait(dve, mean_done, i, t)
                if t == 0:
                    dve.wait_ge(g_landed, 16 * (norm_index[i] + 1))
                    dve.wait_ge(b_landed, 16 * (norm_index[i] + 1))
                return dve.scalar_tensor_tensor(xn[:, t, :], x[:, t, :], nmean[:, t, :], gb[:, 0, :], ALU.add, ALU.mult)

            def scale(i, t):
                wait(dve, rstd_done, i, t)
                for c in range(2):
                    h = slice(c * BLK, (c + 1) * BLK)
                    dve.scalar_tensor_tensor(x[:, t, h], xn[:, t, h], rstd[:, t, :], gb[:, 1, h], ALU.mult,
                                             ALU.add).then_inc(x_new.sem, 1)

            def embed(i, t):
                for c in range(2):
                    if t == 0 and c == 0:
                        wait(dve, sig_done, i)
                    y_wait("ple", i, t, c)
                    h = slice(c * BLK, (c + 1) * BLK)
                    own(dve.tensor_tensor(eg[:, t, h], eg[:, t, h], ps[:, 2 * t + c, :], ALU.mult))
                    dve.tensor_tensor(x[:, t, h], x[:, t, h], eg[:, t, h], ALU.add).then_inc(x_new.sem, 1)

            def boundary(kind, i):
                more = i + 1 < NST
                if kind == "ple":
                    for t in range(NT):
                        embed(i, t)
                        if t == 0:
                            split(2)
                        if more:
                            stream_t("x", i + 1, t)
                    return
                residual(kind, i, 0, 0)
                own(center(i, 0, residual(kind, i, 0, 1)))
                split(1)
                scale(i, 0)
                split(1)
                stream_t("x", i + 1, 0)
                residual(kind, i, 1, 0)
                own(center(i, 1, residual(kind, i, 1, 1)))
                scale(i, 1)
                stream_t("x", i + 1, 1)

            def rotate(dst, bank, n, cs, t):
                c, s, ns = (const(k)[:, t * 32:(t + 1) * 32].unsqueeze(1).broadcast_to((P, n, 32)) for k in cs)
                v = ps[:, bank, 0:n * HD].rearrange("p (h w d) -> p h w d", w=2, d=32)
                a = ra[:, 0:n * HD].rearrange("p (h w d) -> p h w d", w=2, d=32)
                b = rb[:, 0:n * HD].rearrange("p (h w d) -> p h w d", w=2, d=32)
                for w in range(2):
                    dve.tensor_tensor(a[:, :, w, :], v[:, :, w, :], c, ALU.mult)
                dve.tensor_tensor(b[:, :, 0, :], v[:, :, 1, :], ns, ALU.mult)
                own(dve.tensor_tensor(b[:, :, 1, :], v[:, :, 0, :], s, ALU.mult))
                for d in dst:
                    ins = dve.tensor_tensor(d, ra[:, 0:n * HD].rearrange("p (h d) -> p h d", d=HD),
                                            rb[:, 0:n * HD].rearrange("p (h d) -> p h d", d=HD), ALU.add)
                own(ins)
                return ins

            def tokens(kind, what, i, hh, g):
                dve.wait_ge(w_used, ends[what, i, hh, g])
                pair = {"q": 0, "k": 2, "kv": 2, "v": 6}[what]
                if what in ("q", "k", "kv"):
                    for t in range(NT):
                        if kind == "sb":
                            if what == "q":
                                ins = dve.tensor_scalar(qk[:, t, :], ps[:, pair + t, :], HD ** -0.5, None, ALU.mult)
                            else:
                                ins = dve.tensor_copy(qk[:, t, :], ps[:, pair + t, :])
                        elif what == "kv":
                            d = qk[:, t, 0:256].rearrange("p (h w d) -> p h w d", h=2, w=2)
                            rotate([d[:, :, 0, :], d[:, :, 1, :]], pair + t, 2, ("ck", "sk", "nsk"), t)
                        else:
                            rotate([qk[:, t, :].rearrange("p (h d) -> p h d", d=HD)], pair + t, 8,
                                   ("cq", "sq", "nsq") if what == "q" else ("ck", "sk", "nsk"), t)
                    if kind == "sb":
                        ins.then_inc(tok_done.sem, 1)
                    else:
                        dve.sem_inc(tok_done.sem, 1)
                if what == "v":
                    ins = dve.tensor_copy(vv[:, g, :, :], ps[:, pair:pair + 2, :])
                    ins.then_inc(v_done.sem, 1)
                if what == "kv":
                    ins = dve.tensor_copy(vv[:, 0, :, 0:P], ps[:, pair:pair + 2, P:2 * P])
                    ins.then_inc(v_done.sem, 1)

            def softmax_half(kind, i, hh):
                ng = NG if kind == "dil" else 1

                def scores(h, t):
                    n = 2 * h + t
                    wait(dve, acc_ready, "z", i, hh, h, t)
                    w = (t + 1) * ng * P
                    if n >= 2:
                        wait(dve, t_ready, "e", i, hh, h - 1, t)
                    bank = h % 2 if t == 0 else 4
                    z = ps[:, bank:bank + 2, :].rearrange("p b n -> p (b n)")[:, 0:w] if t else ps[:, bank, 0:w]
                    table = const(kind)
                    m = table[:, 0:ng * P] if t == 0 else table[:, ng * P:3 * ng * P]
                    c = t * 8 + h
                    low = const("sink")[:, hh * 8 + h:hh * 8 + h + 1] if kind == "swa" else NEG
                    own(dve.tensor_tensor_reduce(sc[:, n % 2, 0:w], z, m, 1.0, low, ALU.add, ALU.max, nmx[:, 0, c:c + 1]))
                    dve.tensor_scalar(nmx[:, 1, c:c + 1], nmx[:, 0, c:c + 1], -1.0, None, ALU.mult).then_inc(s_done.sem, 1)

                def normalize(h, t):
                    n = 2 * h + t
                    c = t * 8 + h
                    wait(dve, e_done, i, hh, h, t)
                    if kind == "swa":
                        own(dve.tensor_tensor(nmx[:, 2, c:c + 1], nmx[:, 2, c:c + 1], nmx[:, 3, c:c + 1], ALU.add))
                    own(dve.reciprocal(nmx[:, 4, c:c + 1], nmx[:, 2, c:c + 1]))
                    w = (t + 1) * ng * P
                    dve.tensor_scalar(sc[:, n % 2, 0:w], sc[:, n % 2, 0:w], nmx[:, 4, c:c + 1], None, ALU.mult).then_inc(p_done.sem, 1)

                def evac1(h):
                    wait(dve, t_ready, "e", i, hh, h, 1)
                    n = 2 * ng
                    dve.tensor_copy(eT[:, 1, 0:n, :].rearrange("p c m -> p (c m)"),
                                    ps[:, 6:8, :].rearrange("p b n -> p (b n)")[:, 0:n * P]).then_inc(eT1_done.sem, 1)
                scores(0, 0)
                scores(0, 1)
                normalize(0, 0)
                for h in range(HALF):
                    if h + 1 < HALF:
                        scores(h + 1, 0)
                    normalize(h, 1)
                    evac1(h)
                    if h + 1 < HALF:
                        scores(h + 1, 1)
                        normalize(h + 1, 0)

            def stick_half(i, hh):
                def table(name):
                    return const(name).unsqueeze(1).unsqueeze(1).broadcast_to((P, 2, 2, P))

                def soft(h):
                    wait(dve, ln_done, i, hh, h)
                    s = ssp[:, h % 2]
                    own(dve.scalar_tensor_tensor(s, zpair(h), 0.0, sw[:, h % 2], ALU.max, ALU.add))
                    dve.tensor_tensor(diagonals(s), diagonals(s), table("keep"), ALU.mult).then_inc(sp_done.sem, 1)

                def diag(h):
                    wait(dve, cum_done, i, hh, h)
                    dve.tensor_tensor(diagonals(sa[:, h % 2]), diagonals(zpair(h)), table("kill"), ALU.add).then_inc(dm_done.sem, 1)
                soft(0)
                for h in range(PAIRS):
                    if hh == 0:
                        split(1)
                    if h + 1 < PAIRS:
                        soft(h + 1)
                    diag(h)

            def mix(l, i):
                kind = mixer_of(l)
                for what, hh, g in triples_of(l):
                    if what == "attn":
                        if hh == 1:
                            wait(dve, th_done, "o", i, 0)
                            dve.tensor_tensor(xl[:, 0:4], o, xh[:, 0:4].bitcast(F32), ALU.subtract).then_inc(tl_done.sem, 1)
                        stick_half(i, hh) if kind == "sb" else softmax_half(kind, i, hh)
                        if hh == 1:
                            wait(dve, th_done, "o", i, 1)
                            dve.tensor_tensor(xl[:, 4:8], oall, xh[:, 4:8].bitcast(F32), ALU.subtract).then_inc(tl_done.sem, 1)
                        continue
                    if not (kind == "sb" and (what, hh) == ("q", 1)):
                        split(units_of(what))
                    tokens(kind, what, i, hh, g)
                split(4)

            def ple(i):
                split(2)
                wait(dve, th_done, "p", i)
                dve.tensor_tensor(ptl[:], ps[:, 0, :].rearrange("p (c t m) -> p c t m", c=2, t=NT), pth[:].bitcast(F32),
                                  ALU.subtract).then_inc(tl_done.sem, 1)
                split(4)

            dve.wait_ge(c_landed, 16)
            dve.wait_ge(p_landed, 16)
            split(LEAD)
            for t in range(NT):
                stream_t("x", 0, t)
            for kind, l, i, u0, n in stages:
                assert st["u"] == u0 + LEAD, (kind, st["u"], u0)
                if kind in ("ffn1", "ffn2"):
                    ffn(i)
                elif kind == "mix":
                    mix(l, i)
                else:
                    ple(i)
                split(2)
                boundary(kind, i)

        @block.tensor
        def _(pe):
            st = {"u": 0}

            def three(out_, a_h, a_l, u, k, ncol, start, stop, cols=None):
                b_h = view(wh, u % RING, ncol)[:, k, :]
                b_l = view(wl, u % RING, ncol)[:, k, :]
                pe.matmul(out_, a_h, b_h, start=start, stop=False)
                pe.matmul(out_, a_h, b_l, start=False, stop=False)
                return pe.matmul(out_, a_l, b_h, start=False, stop=stop)

            def unit(u, t, bank, chunk0, ncol, ah, al, start, stop):
                nk = UW // ncol
                for k in range(nk):
                    ins = three(ps[:, bank, 0:ncol], ah[:, chunk0 + k, t, :], al[:, chunk0 + k, t, :], u, k, ncol,
                                start and k == 0, stop and k == nk - 1)
                return ins

            def ready(u, du=0):
                pe.wait_ge(lo_done, u + 1 + du)

            def run(items, by_tile, between=None, du=0, y=(), before=None):
                u = st["u"]
                st["u"] += len(items)
                if by_tile:
                    for t in range(NT):
                        if t and between:
                            between()
                        for n, it in enumerate(items):
                            if t == 0:
                                ready(u + n, du)
                            if before:
                                before(t, n)
                            ins = unit(u + n, t, *it(t))
                            if t == NT - 1:
                                ins.then_inc(w_used, 1)
                            elif n in y:
                                ins.then_inc(acc_ready.sem, 1)
                else:
                    for n, it in enumerate(items):
                        ready(u + n, du)
                        for t in range(NT):
                            if before:
                                before(t, n)
                            ins = unit(u + n, t, *it(t))
                        ins.then_inc(w_used, 1)

            def transposes(src, n, bank, t, at=0):
                for c in range(n):
                    ins = pe.transpose(ps[:, bank + c // 4, (c % 4) * P:(c % 4 + 1) * P], src[:, at + c * P:at + (c + 1) * P], ident)
                return ins

            def stream_t(key, i, t):
                for c in range(2):
                    if i:
                        wait(pe, x_new, i - 1, t, c)
                    else:
                        pe.wait_ge(x_landed, 16)
                    transposes(x[:, t, :], 4, 2 * t + c, t, c * BLK).then_inc(t_ready.sem, 1)

            def y_items(nunits, ah, al, banks=lambda t, c: 4 + 2 * t + c, n0=0, chunk0=0, first=True, last=True):
                items = []
                for n in range(nunits):
                    k, c = n // 2, n % 2
                    items.append(lambda t, k=k, c=c: (banks(t, c), chunk0 + 2 * k, BLK, ah, al, first and k == 0,
                                                      last and k == nunits // 2 - 1))
                return items

            def col_items(pair, ncol, ah=xh, al=xl):
                nk = UW // ncol
                n = 8 // nk
                return [lambda t, m=m: (pair + t, m * nk, ncol, ah, al, m == 0, m == n - 1) for m in range(n)]

            def hidden_t(i, j, n, dj=0):
                pe.wait_ge(h_done.sem, h_done.at(i, j) + dj)
                for t in range(NT):
                    ins = transposes(hb[:, t, :], n, 2 + t, t)
                ins.then_inc(t_ready.sem, 1)

            def halves(key, i, first_of_half):
                def f(t, n):
                    if n == 0:
                        wait(pe, tl_done, key, i, t, 0)
                    if n == first_of_half:
                        wait(pe, tl_done, key, i, t, 1)
                return f

            def second(i, key="x"):
                return lambda: stream_t(key, i, 1)

            def ffn(i):
                stream_t("x", i, 0)
                run(col_items(0, BLK), True, second(i), before=halves("x", i, 2))
                run(col_items(2, BLK), False)
                def block_of(j, dj, first):
                    du = 12 * dj
                    g = col_items(0, BLK)
                    pe.wait_ge(silu_done.sem, silu_done.at(i, j - 1) + dj)
                    run(g[0:3], False, du=du)
                    hidden_t(i, j - 1, 4, dj)
                    run(g[3:4], False, du=du)
                    pe.wait_ge(tl_done.sem, tl_done.at("h", i, j - 1) + dj)
                    run(y_items(4, hth, htl, first=first, last=False), False, du=du)
                    run(col_items(2, BLK), False, du=du)

                block_of(1, 0, True)
                with pe.Fori(0, NJ - 2) as r:
                    block_of(2, r, False)
                st["u"] += 12 * (NJ - 3)
                g = col_items(0, 256)
                wait(pe, silu_done, i, NJ - 1)
                run(g[0:1], False)
                hidden_t(i, NJ - 1, 4)
                run(g[1:2], False)
                wait(pe, tl_done, "h", i, NJ - 1)
                run(col_items(2, 256), False)
                down = y_items(4, hth, htl, first=False, last=False)
                run(down[0:1], False)
                hidden_t(i, NJ, 2)
                run(down[1:2], False)
                last = y_items(2, hth, htl, chunk0=4, first=False)
                run([down[2], last[0], down[3], last[1]], True, y=(1, 3),
                    before=lambda t, n: wait(pe, tl_done, "h", i, NJ) if (t, n) == (0, 1) else None)

            def attn_z(i, hh, h, t, ng, kc):
                pb = HD * (h % 2)
                for g in range(ng):
                    bank = h % 2 if t == 0 else 4 + (g * 256) // BLK
                    at = (g * (t + 1) * P) % BLK
                    ins = pe.matmul(ps[:, bank, at:at + (t + 1) * P], qT[pb:pb + HD, g, h // 2, t * P:(t + 1) * P],
                                    kT[pb:pb + HD, g, h // 2 if kc is None else kc, 0:(t + 1) * P], start=True, stop=True)
                ins.then_inc(acc_ready.sem, 1)

            def softmax_half(kind, i, hh):
                ng = NG if kind == "dil" else 1
                kc = None if kind == "dil" else hh
                order = [(h, t) for h in range(HALF) for t in range(NT)]

                def z(n):
                    h, t = order[n]
                    if t == 0 and h >= 2:
                        wait(pe, s_done, i, hh, h - 2, 0)
                    if t == 1 and h >= 1:
                        wait(pe, s_done, i, hh, h - 1, 1)
                    attn_z(i, hh, h, t, ng, kc)

                def tr(n):
                    h, t = order[n]
                    wait(pe, p_done, i, hh, h, t)
                    transposes(sc[:, n % 2, :], ng * (t + 1), 6, t).then_inc(t_ready.sem, 1)

                def av(n):
                    h, t = order[n]
                    wait(pe, (eT0_done, eT1_done)[t], i, hh, h)
                    m = 0
                    for g in range(ng):
                        for kb in range(t + 1):
                            v = vv[:, g, kb, h * HD:(h + 1) * HD] if kind == "dil" else vv[:, 0, kb, hh * HD:(hh + 1) * HD]
                            pb = HD * (h % 2)
                            ins = pe.matmul(opair(h)[pb:pb + HD, t * P:(t + 1) * P], v, eT[:, t, m, :],
                                            start=m == 0, stop=m == ng * (t + 1) - 1)
                            m += 1
                    return ins
                z(0)
                for n in range(len(order)):
                    if n + 1 < len(order):
                        z(n + 1)
                    if n:
                        av(n - 1)
                    tr(n)
                av(len(order) - 1).then_inc(acc_ready.sem, 1)

            def stick_half(i, hh, filler):
                def z(h):
                    for m in range(2):
                        pb = HD * m
                        q, k = qT[pb:pb + HD, 0, h, :], kT[pb:pb + HD, 0, h, :]
                        pe.matmul(zpair(h)[:, m, 0:S], k[:, 0:P], q, start=True, stop=False)
                        ins = pe.matmul(zpair(h)[:, m, S:S + P], k[:, P:S], q[:, P:S], start=False, stop=True)
                    ins.then_inc(acc_ready.sem, 1)

                def cum(h):
                    wait(pe, sp_done, i, hh, h)
                    for m in range(2):
                        pe.matmul(zpair(h)[:, m, :], const("lower"), ssp[:, h % 2, m, :], start=False, stop=False, skip_group_check=True)
                        ins = pe.matmul(zpair(h)[:, m, P:2 * P], const("ones"), ssp[:, h % 2, m, 2 * P:3 * P], start=False,
                                        stop=True, skip_group_check=True)
                    ins.then_inc(cum_done.sem, 1)

                def av(h):
                    wait(pe, a_done, i, hh, h)
                    for m in range(2):
                        a = sa[:, h % 2, m, :]
                        c = slice((2 * h + m) * HD, (2 * h + m + 1) * HD)
                        out_ = opair(2 * h)[HD * m:HD * (m + 1), :]
                        pe.matmul(out_, vv[:, 0, 0, c], a[:, 0:S], start=True, stop=False)
                        ins = pe.matmul(out_[:, P:S], vv[:, 0, 1, c], a[:, S:S + P], start=False, stop=True)
                    return ins
                z(0)
                z(1)
                for h in range(PAIRS):
                    if filler:
                        run(filler[h:h + 1], False)
                    cum(h)
                    if h:
                        av(h - 1)
                    if h and h + 1 < PAIRS:
                        z(h + 1)
                av(PAIRS - 1).then_inc(acc_ready.sem, 1)

            def mix(l, i):
                kind = mixer_of(l)
                stream_t("x", i, 0)
                pending = None
                steps = triples_of(l)

                def head_t(what, hh, g):
                    wait(pe, tok_done, what, i, hh, g)
                    for t in range(NT):
                        ins = transposes(qk[:, t, :], 2 if what == "kv" else 4, 4 + t, t)
                    ins.then_inc(t_ready.sem, 1)
                first = True
                filled = False
                used = {}
                copied = None
                for what, hh, g in steps:
                    if what == "attn":
                        if pending:
                            if copied:
                                wait(pe, th_done, *copied)
                            head_t(*pending)
                            copied = (pending[0], i, pending[1], pending[2])
                            pending = None
                        wait(pe, th_done, *copied)
                        wait(pe, v_done, i, 0 if kind == "swa" else hh, NG - 1 if kind == "dil" else 0)
                        used = {}
                        if kind == "sb":
                            stick_half(i, hh, col_items(0, BLK) if hh == 0 else [])
                            if hh == 0:
                                used[0], pending, filled = ("q", i, 1, 0), ("q", 1, 0), True
                        else:
                            softmax_half(kind, i, hh)
                        continue
                    if filled:
                        filled = False
                        continue
                    pair = {"q": 0, "k": 2, "kv": 2, "v": 6}[what]
                    if pair == 2 and hh == 1 and g == 0:
                        wait(pe, o_done, i)
                    if pair in used:
                        if pair == 6:
                            wait(pe, v_done, *used[pair])
                        else:
                            wait(pe, tok_done, *used[pair])
                    used[pair] = (i, hh, g) if what == "v" else (what, i, hh, g)
                    items = col_items(pair, 256 if what == "kv" else BLK)
                    if first:
                        run(items, True, second(i), before=halves("x", i, 2))
                        first = False
                    else:
                        run(items[:-1], False)
                        if pending:
                            if copied:
                                wait(pe, th_done, *copied)
                            head_t(*pending)
                            copied = (pending[0], i, pending[1], pending[2])
                            pending = None
                        run(items[-1:], False)
                    if what != "v":
                        pending = (what, hh, g)
                wait(pe, tl_done, "o", i, 0)
                y = y_items(8, xh, xl)
                run(y[0:4], False)
                wait(pe, tl_done, "o", i, 1)
                run([y[4], y[6], y[5], y[7]], True, y=(1, 3))

            def ple(l, i):
                stream_t("x", i, 0)
                y = y_items(8, xh, xl)
                run(y[0:4], True, second(i), before=halves("x", i, 3))
                pe.wait_ge(p_landed, 16 * (l + 2))
                for t in range(NT):
                    for c in range(2):
                        ins = pe.transpose(ps[:, 0, (2 * c + t) * P:(2 * c + t + 1) * P], pin[:, t, c * P:(c + 1) * P], ident)
                ins.then_inc(t_ready.sem, 1)
                run(y[4:6], False)
                pr = y_items(2, pth, ptl, banks=lambda t, c: 2 * t + c)
                run(y[6:8], False)
                wait(pe, tl_done, "p", i)
                run(pr, True, y=(0, 1))

            pe.wait_ge(c_landed, 16)
            for kind, l, i, u0, n in stages:
                assert st["u"] == u0, (kind, st["u"], u0)
                if kind in ("ffn1", "ffn2"):
                    ffn(i)
                elif kind == "mix":
                    mix(l, i)
                else:
                    ple(l, i)


def constants():
    import numpy as np
    t = np.zeros((P, CONST["sink"][0]), np.float32)

    def put(name, v):
        a, b = CONST[name]
        t[:, a:b] = v
    p, q = np.arange(P)[:, None], np.arange(P)[None, :]
    put("ident", p == q)
    put("lower", -1.0 * (p >= q))
    put("ones", -1.0)
    put("keep", p < q)
    put("kill", np.where(p < q, 0.0, NEG))
    key = np.arange(S)[None, :]

    def banded(ok):
        return [np.where(ok(t * P + p - key[:, 0:(t + 1) * P]), 0.0, NEG) for t in range(NT)]
    put("swa", np.concatenate(banded(lambda d: (d >= 0) & (d <= 127)), 1))
    per = [banded(lambda d, w=w, s=s: (d >= 0) & (d % s == 0) & (d // s <= w // s)) for w, s in DIL]
    put("dil", np.concatenate([m[t] for t in range(NT) for m in per], 1))
    pos = np.arange(S, dtype=np.float32)
    inv = np.float32(10000.0) ** (-np.arange(0, HD, 2, dtype=np.float32) / np.float32(HD))
    ang = (pos[:, None] * inv[None, :]).astype(np.float32)
    c, s = np.cos(ang), np.sin(ang)
    rows = lambda m: np.concatenate([m[0:P], m[P:S]], 1)
    for name, m in (("cq", c * HD ** -0.5), ("sq", s * HD ** -0.5), ("nsq", -s * HD ** -0.5), ("ck", c), ("sk", s), ("nsk", -s)):
        put(name, rows(m))
    return t


_INS = ['x', 'p', 'ffn1_w_in', 'ffn1_w_out', 'ffn2_w_in', 'ffn2_w_out', 'ln_g', 'ln_b', 'sb_w_in', 'sb_w_out',
        'swa_w_in', 'swa_sinks', 'swa_w_out', 'dil_w_in', 'dil_w_out', 'ple_w_proj', 'ple_w_gate']


def kernel(**inputs):
    import numpy as np
    import concourse.bacc as bacc
    from concourse.bass_utils import run_bass_kernel_spmd

    nc = bacc.Bacc("TRN2", target_bir_lowering=False, num_devices=1)
    arrays, aps = {}, {}
    for name in _INS:
        arrays[f"in_{name}"] = np.ascontiguousarray(inputs[name])
    arrays["in_consts"] = constants()
    for name in _INS + ["consts"]:
        a = arrays[f"in_{name}"]
        aps[name] = nc.dram_tensor(f"in_{name}", a.shape, mybir.dt.from_np(a.dtype), kind="ExternalInput").ap()
    out = nc.dram_tensor("out_dram", (1, S, D), F32, kind="ExternalOutput").ap()
    build_program(nc, aps, out)
    r = run_bass_kernel_spmd(nc, [arrays], core_ids=[0])
    return r.results[0]["out_dram"]
```

```python
from contextlib import ExitStack

import concourse.bass as bass
from concourse import mybir

F32 = mybir.dt.float32
F32R = mybir.dt.float32r
I32 = mybir.dt.int32
ALU = mybir.AluOpType
ACT = mybir.ActivationFunctionType

P = 128
D = 1024
S = 256
NT = S // P
DEPTH = 4
FF = 2816
PLE = 256
HD = 64
HALF = 8
PAIRS = HALF // 2
ALPHA = (2 * DEPTH) ** 0.25
EPS = 1e-5
NEG = -1e30
RING = 6
LEAD = 4
UW = 1024
BLK = 512
NJ = FF // BLK
DIL = ((128, 1), (512, 4), (2048, 16))
NG = len(DIL)

CONST = {}
_at = 0
for _name, _n in (("ident", P), ("lower", P), ("ones", P), ("kill", 2 * P), ("swa", 3 * P),
                  ("dil", 3 * NG * P), ("cq", 64), ("sq", 64), ("nsq", 64), ("ck", 64), ("sk", 64), ("nsk", 64),
                  ("sink", 16)):
    CONST[_name] = (_at, _at + _n)
    _at += _n
CONST_W = _at


def mixer_of(l):
    return ("sb", "swa", "dil")[l % 3]


class Signal:

    def __init__(self, sem):
        self.sem, self.place = sem, {}

    def note(self, *key):
        self.place[key] = len(self.place) + 1

    def at(self, *key):
        return self.place[key]


def steps_of(l):
    kind = mixer_of(l)
    if kind == "swa":
        return [("q", 0, 0), ("kv", 0, 0), ("q", 1, 0), ("attn", 0, 0), ("attn", 1, 0)]
    steps = []
    for hh in range(2):
        for g in range(NG if kind == "dil" else 1):
            steps += [("q", hh, g), ("k", hh, g), ("v", hh, g)]
        steps.append(("attn", hh, 0))
    return steps


def bank_of(kind, what, hh):
    if kind == "swa":
        return {"q": (0, 2)[hh], "kv": 6}[what]
    return {"q": 0, "k": 2, "v": 0 if (kind, hh) == ("sb", 1) else 6}[what]


def units_of(step):
    return 2 if step == "kv" else 4


def build_program(nc, A, out):
    ctx = ExitStack()
    with ctx:
        def sb(name, shape, dt=F32):
            return ctx.enter_context(nc.sbuf_tensor(name, shape, dt))

        raw = sb("raw", [P, RING, UW])
        wh = sb("wh", [P, RING, UW], F32R)
        wl = sb("wl", [P, RING, UW], F32R)
        x = sb("x", [P, NT, D])
        xh = sb("xh", [P, D // P, NT, P], F32R)
        xl = sb("xl", [P, D // P, NT, P], F32R)
        hth = sb("hth", [P, 6, NT, P], F32R)
        htl = sb("htl", [P, 6, NT, P], F32R)
        pth = sb("pth", [P, 2, NT, P], F32R)
        ptl = sb("ptl", [P, 2, NT, P], F32R)
        pin = sb("pin", [P, NT, PLE])
        gb = sb("gb", [P, 2, D])
        consts = sb("consts", [P, CONST_W])
        ident_r = sb("ident_r", [P, P], F32R)
        kill_r = sb("kill_r", [P, 2, P], F32R)
        rsum = sb("rsum", [P, NT, 2])
        nmean = sb("nmean", [P, NT, 1])
        ssq = sb("ssq", [P, NT, 1])
        veps = sb("veps", [P, NT, 1])
        rstd = sb("rstd", [P, NT, 1])
        mhalf = sb("mhalf", [P, 1])
        nmx = sb("nmx", [P, 4, 2 * HALF])
        nsink = sb("nsink", [P, 16])
        arena = sb("arena", [P, 16896])
        place = [0]

        def part(n):
            place[0] += n
            return arena[:, place[0] - n:place[0]]

        qT = part(NG * 4 * S).rearrange("p (g c s) -> p g c s", g=NG, c=4)
        kT = part(NG * 4 * S).rearrange("p (g c s) -> p g c s", g=NG, c=4)
        vv = part(NG * NT * BLK).rearrange("p (g t n) -> p g t n", g=NG, t=NT)
        qk = part(NT * BLK).rearrange("p (t n) -> p t n", t=NT)
        ra = part(BLK)
        rb = part(BLK)
        sc = part(3 * 3 * NG * P).rearrange("p (b n) -> p b n", b=3)
        eT = part(3 * NG * P).rearrange("p (m q) -> p m q", q=P)
        o = part(4 * S).rearrange("p (c t m) -> p c t m", c=4, t=NT)
        sg = arena[:, 0:NT * BLK].rearrange("p (t n) -> p t n", t=NT)
        hb = arena[:, NT * BLK:2 * NT * BLK].rearrange("p (t n) -> p t n", t=NT)
        eg = arena[:, 0:NT * D].rearrange("p (t n) -> p t n", t=NT)
        xn = arena[:, 0:NT * D].rearrange("p (t n) -> p t n", t=NT)
        sq = arena[:, NT * D:NT * D + D]
        kvt = kT[:, 1:3].rearrange("p g c s -> p (g c s)")[:, 0:NT * 256].rearrange("p (t n) -> p t n", t=NT)
        def pair_buffer(of):
            v = of[:, 1:3].rearrange("p g c s -> p (g c s)")[:, 0:4 * 384]
            return v.rearrange("p (b h n) -> p b h n", b=2, h=2)
        sw = pair_buffer(qT)
        ssp = pair_buffer(kT)
        sa = pair_buffer(vv)

        ps = ctx.enter_context(nc.psum_tensor("ps", [P, 8, BLK], F32))

        def zpair(h):
            b = (4, 6)[h % 2]
            return ps[:, b:b + 2, 0:384]

        def opair(h):
            return ps[:, 2 + h // 4, (h // 2) % 2 * S:((h // 2) % 2 + 1) * S]

        oall = ps[:, 2:4, :].rearrange("p b (c t m) -> p (b c) t m", c=2, t=NT)

        def of_tile(t, ng):
            return slice(t * ng * P, (1 + 2 * t) * ng * P)

        def const(name):
            a, b = CONST[name]
            return consts[:, a:b]

        ident = const("ident")

        def signal(name):
            return Signal(ctx.enter_context(nc.semaphore(name)))

        def semaphore(name):
            return ctx.enter_context(nc.semaphore(name))

        landed = [semaphore(f"landed{s}") for s in range(RING)]
        hi_done = semaphore("hi_done")
        lo_done = semaphore("lo_done")
        w_used = semaphore("w_used")
        x_landed = [semaphore(f"x_landed{t}") for t in range(NT)]
        i_landed = semaphore("i_landed")
        c_landed = semaphore("c_landed")
        g_landed = semaphore("g_landed")
        b_landed = semaphore("b_landed")
        p_landed = semaphore("p_landed")
        stored = [semaphore(f"stored{t}") for t in range(NT)]
        acc_ready = signal("acc_ready")
        t_ready = signal("t_ready")
        th_done = signal("th_done")
        tl_done = signal("tl_done")
        silu_done = signal("silu_done")
        h_done = signal("h_done")
        x_new = signal("x_new")
        mean_done = signal("mean_done")
        xn_done = signal("xn_done")
        ssq_done = signal("ssq_done")
        rstd_done = signal("rstd_done")
        tok_done = signal("tok_done")
        v_done = signal("v_done")
        s_done = signal("s_done")
        e_done = signal("e_done")
        p_done = signal("p_done")
        eT_done = signal("eT_done")
        ln_done = signal("ln_done")
        sp_done = signal("sp_done")
        cum_done = signal("cum_done")
        a_done = signal("a_done")
        o_done = signal("o_done")
        sig_done = signal("sig_done")
        own_act = semaphore("own_act")
        own_dve = semaphore("own_dve")
        mh_done = semaphore("mh_done")
        masks_done = semaphore("masks_done")

        stages = []
        u = 0
        for l in range(DEPTH):
            for kind in ("ffn1", "mix", "ffn2", "ple"):
                n = {"ffn1": 66, "ffn2": 66, "ple": 10, "mix": 8 + sum(units_of(s[0]) for s in steps_of(l) if s[0] != "attn")}[kind]
                stages.append((kind, l, len(stages), u, n))
                u += n
        UNITS = u
        NST = len(stages)

        ends = {}
        def note_stream(key, i):
            for t in range(NT):
                for c in range(2):
                    t_ready.note(key, i, t, c), th_done.note(key, i, t, c), tl_done.note(key, i, t, c)

        note_stream("x", 0)
        for kind, l, i, u0, n in stages:
            if kind in ("ffn1", "ffn2"):
                for j in range(NJ + 1):
                    base = u0 if j == 0 else u0 + 8 + 12 * (j - 1)
                    ends["gate", i, j] = base + (4 if j < NJ else 2)
                    ends["up", i, j] = base + (8 if j == 0 else 12 if j < NJ else 4)
                    silu_done.note(i, j), h_done.note(i, j)
                    t_ready.note("h", i, j), th_done.note("h", i, j), tl_done.note("h", i, j)
            elif kind == "mix":
                at = u0
                for what, hh, g in steps_of(l):
                    if what != "attn":
                        at += units_of(what)
                        ends[what, i, hh, g] = at
                        if what != "v":
                            tok_done.note(what, i, hh, g)
                            th_done.note(what, i, hh, g)
                            if (mixer_of(l), hh) != ("swa", 1):
                                t_ready.note(what, i, hh, g)
                        if what in ("v", "kv"):
                            v_done.note(i, hh, g)
                    elif mixer_of(l) == "sb":
                        for h in range(PAIRS):
                            for one in (ln_done, sp_done, cum_done, a_done):
                                one.note(i, hh, h)
                            acc_ready.note("z", i, hh, h)
                        acc_ready.note("o", i, hh)
                    else:
                        for h in range(HALF):
                            for t in range(NT):
                                acc_ready.note("z", i, hh, h, t), s_done.note(i, hh, h, t), e_done.note(i, hh, h, t)
                                t_ready.note("e", i, hh, h, t)
                                p_done.note(i, hh, h, t), eT_done.note(i, hh, h, t)
                        if (mixer_of(l), hh) == ("swa", 0):
                            t_ready.note("q", i, 1, 0)
                        acc_ready.note("o", i, hh)
                o_done.note(i)
                for c in range(2):
                    th_done.note("o", i, c), tl_done.note("o", i, c)
            else:
                ends["gate", i] = u0 + 8
                t_ready.note("p", i), th_done.note("p", i), tl_done.note("p", i), acc_ready.note("gate", i)
                for t in range(NT):
                    sig_done.note(i, t)
            ends["y", i] = u0 + n
            acc_ready.note("y", i, 0), acc_ready.note("y", i, 1)
            for t in range(NT):
                x_new.note(i, t, 0), x_new.note(i, t, 1)
                if kind != "ple":
                    mean_done.note(i, t), xn_done.note(i, t), ssq_done.note(i, t), rstd_done.note(i, t)
            if i + 1 < NST:
                note_stream("x", i + 1)

        norm_index = {i: 3 * l + ("ffn1", "mix", "ffn2").index(kind) for kind, l, i, _, _ in stages if kind != "ple"}

        def wait(eng, sig, *key):
            eng.wait_ge(sig.sem, sig.at(*key))

        def view(ring, slot, ncol):
            return ring[:, slot, :].rearrange("p (k n) -> p k n", n=ncol)

        block = ctx.enter_context(nc.Block())

        @block.sync
        def _(sp):
            st = {"u": 0}

            def load(src, rows, cols, ncol, base=None):
                u = st["u"]
                st["u"] += 1
                if u >= RING:
                    sp.wait_ge(lo_done, u - RING + 1 + (0 if base is None else base))
                nk = UW // ncol
                v = src.rearrange("(k p) n -> p k n", p=P)
                sp.dma_start(view(raw, u % RING, ncol),
                             v[:, bass.ds(rows, nk), bass.ds(cols, ncol)]).then_inc(landed[u % RING], 16)

            def ffn(l, i, win, wout):
                def block_of(j, base, first=False):
                    for k in range(0, 8, 2):
                        load(win, k, j * BLK, BLK, base)
                        if first and i == 0 and k == 2:
                            load_x(1)
                    if not first:
                        for k in range(2):
                            for c in range(2):
                                load(wout, j * 4 - 4 + 2 * k, c * BLK, BLK, base)
                    for k in range(0, 8, 2):
                        load(win, k, j * BLK + FF, BLK, base)
                block_of(0, None, True)
                if i == 0:
                    sp.dma_start(consts[:, P:CONST["sink"][0]], A["consts"][:, P:]).then_inc(c_landed, 16)
                    sp.dma_start(const("sink"), A["swa_sinks"][0].partition_broadcast(P)).then_inc(p_landed, 16)
                norm_load(i)
                with sp.Fori(0, NJ - 1) as r:
                    block_of(r + 1, r * 12)
                st["u"] += 12 * (NJ - 2)
                for c in (NJ * BLK, NJ * BLK + FF):
                    for k in (0, 4):
                        load(win, k, c, 256)
                down = [(NJ * 4 - 4 + 2 * k, c) for k in range(3) for c in range(2)]
                for k, c in down[0:2] + sorted(down[2:6], key=lambda kc: kc[1]):
                    load(wout, k, c * BLK, BLK)

            def load_x(t):
                sp.dma_start(x[:, t, :], A["x"][0].rearrange("(t p) n -> p t n", p=P)[:, t, :]).then_inc(x_landed[t], 16)

            def norm_load(i):
                n = norm_index[i]
                if n:
                    before = i - 1 if i - 1 in norm_index else i - 2
                    wait(sp, x_new, before, 1, 1)
                sp.dma_start(gb[:, 0, :], A["ln_g"].rearrange("l k n -> (l k) n")[n].partition_broadcast(P)).then_inc(g_landed, 16)
                sp.dma_start(gb[:, 1, :], A["ln_b"].rearrange("l k n -> (l k) n")[n].partition_broadcast(P)).then_inc(b_landed, 16)

            sp.dma_start(ident, A["consts"][:, 0:P]).then_inc(i_landed, 16)
            load_x(0)
            for kind, l, i, u0, n in stages:
                assert st["u"] == u0, (kind, st["u"], u0)
                if kind == "ffn1":
                    ffn(l, i, A["ffn1_w_in"][l], A["ffn1_w_out"][l])
                elif kind == "ffn2":
                    ffn(l, i, A["ffn2_w_in"][l], A["ffn2_w_out"][l])
                elif kind == "mix":
                    name = mixer_of(l)
                    win, wout = A[f"{name}_w_in"][l // 3], A[f"{name}_w_out"][l // 3]
                    for n, (what, hh, g) in enumerate(steps_of(l)):
                        if n == 2:
                            norm_load(i)
                        if what == "kv":
                            for k in (0, 4):
                                load(win, k, D, 256)
                        elif what != "attn":
                            col = g * 3 * D + "qkv".index(what) * D + hh * BLK
                            for k in range(0, 8, 2):
                                load(win, k, col, BLK)
                    y = [(k, c) for k in range(0, 8, 2) for c in range(2)]
                    for k, c in y[0:4] + sorted(y[4:8], key=lambda kc: kc[1]):
                        load(wout, k, c * BLK, BLK)
                else:
                    if l:
                        wait(sp, t_ready, "p", i - 4)
                    sp.dma_start(pin[:], A["p"][l, 0].rearrange("(t p) n -> p t n", p=P)).then_inc(p_landed, 16)
                    for k in range(0, 8, 2):
                        for c in range(2):
                            load(A["ple_w_gate"][l], k, c * BLK, BLK)
                    for c in range(2):
                        load(A["ple_w_proj"][l], 0, c * BLK, BLK)
            for t in range(NT):
                wait(sp, x_new, NST - 1, t, 1)
                sp.dma_start(out[0].rearrange("(t p) n -> p t n", p=P)[:, t, :], x[:, t, :]).then_inc(stored[t], 16)
            for t in range(NT):
                sp.wait_ge(stored[t], 16)

        @block.gpsimd
        def _(pool):
            pool.memset(mhalf[:], -0.5).then_inc(mh_done, 1)
            pool.wait_ge(mh_done, 1)
            for kind, l, i, u0, n in stages:
                if kind != "ple":
                    for t in range(NT):
                        wait(pool, ssq_done, i, t)
                        pool.tensor_scalar(veps[:, t, :], ssq[:, t, :], 1.0 / D, EPS, ALU.mult, ALU.add).then_inc(mh_done, 1)
                        pool.wait_ge(mh_done, 2 + 2 * norm_index[i] + t)
                        pool.tensor_tensor(rstd[:, t, :], veps[:, t, :], mhalf[:], ALU.pow).then_inc(rstd_done.sem, 1)
                        if t == 0:
                            for u in (u0 + n + LEAD - 2, u0 + n + LEAD - 1):
                                pool.wait_ge(hi_done, u + 1)
                                pool.wait_ge(lo_done, u)
                                pool.tensor_tensor(wl[:, u % RING, :], raw[:, u % RING, :], wh[:, u % RING, :].bitcast(F32),
                                                   ALU.subtract).then_inc(lo_done, 1)

        @block.scalar
        def _(act):
            st = {"u": 0, "own": 0}

            def own(ins):
                st["own"] += 1
                ins.then_inc(own_act, 1)
                act.wait_ge(own_act, st["own"])

            def split(n=1, loop=None):
                for _ in range(n):
                    u = st["u"]
                    if u >= UNITS:
                        return
                    st["u"] += 1
                    du, dr = loop or (0, 0)
                    act.wait_ge(landed[u % RING], 16 * (u // RING + 1) + dr)
                    if u >= RING:
                        act.wait_ge(w_used, u - RING + 1 + du)
                    act.activation(wh[:, u % RING, :], raw[:, u % RING, :], ACT.Copy).then_inc(hi_done, 1)

            def stream_t(key, i, t):
                for c in range(2):
                    wait(act, t_ready, key, i, t, c)
                    act.activation(xh[:, 4 * c:4 * c + 4, t, :], ps[:, 2 * t + c, :].rearrange("p (k m) -> p k m", m=P),
                                   ACT.Copy).then_inc(th_done.sem, 1)

            def hidden_t(i, j, n, at, dj=0):
                act.wait_ge(t_ready.sem, t_ready.at("h", i, j) + dj)
                for t in range(NT):
                    ins = act.activation(hth[:, at:at + n, t, :], ps[:, 2 + t, 0:n * P].rearrange("p (c m) -> p c m", m=P), ACT.Copy)
                ins.then_inc(th_done.sem, 1)

            def silu(i, j, n, dj=0):
                act.wait_ge(w_used, ends["gate", i, j] + 12 * dj)
                for t in range(NT):
                    ins = act.activation(sg[:, t, 0:n], ps[:, t, 0:n], ACT.Silu)
                ins.then_inc(silu_done.sem, 1)

            def ffn(i):
                split(8 - 4)
                silu(i, 0, BLK)
                split(4)
                with act.Fori(0, NJ - 1) as r:
                    lp = (r * 12, r * 32)
                    split(3, lp)
                    hidden_t(i, 0, 4, 0, r)
                    split(2, lp)
                    silu(i, 1, BLK, r)
                    split(7, lp)
                st["u"] += 12 * (NJ - 2)
                split(2)
                hidden_t(i, NJ - 1, 4, 0)
                silu(i, NJ, 256)
                split(4)
                hidden_t(i, NJ, 2, 4)

            def boundary(kind, i):
                if kind == "ple":
                    split(1)
                    act.wait_ge(w_used, ends["gate", i])
                    sigmoid(i, 1)
                    split(1)
                for t in range(NT):
                    if kind != "ple":
                        wait(act, mean_done, i, t)
                        act.activation(sq, x[:, t, :], ACT.Square, bias=nmean[:, t, :], accum_out=ssq[:, t, :]).then_inc(ssq_done.sem, 1)
                    if i + 1 < NST:
                        if t == 0 and kind != "ple":
                            split(2)
                        stream_t("x", i + 1, t)

            def copy_t(kind, i, what, hh, g):
                wait(act, t_ready, what, i, hh, g)
                n = 2 if what == "kv" else 4
                dst = kT[:, g] if what != "q" else qT[:, hh if kind == "swa" else g]
                for t in range(NT):
                    ins = act.activation(dst[:, 0:n, t * P:(t + 1) * P],
                                         ps[:, 4 + t, 0:n * P].rearrange("p (c m) -> p c m", m=P), ACT.Copy)
                ins.then_inc(th_done.sem, 1)

            def softmax_half(kind, i, hh):
                ng = NG if kind == "dil" else 1

                def exps(h):
                    for t in range(NT):
                        wait(act, s_done, i, hh, h, t)
                        w = of_tile(t, ng)
                        c = 2 * h + t
                        if kind == "swa":
                            act.activation(nmx[:, 2, c:c + 1], const("sink")[:, hh * HALF + h:hh * HALF + h + 1], ACT.Exp,
                                           bias=nmx[:, 0, c:c + 1])
                        act.activation(sc[:, h % 3, w], sc[:, h % 3, w], ACT.Exp, bias=nmx[:, 0, c:c + 1], scale=-1.0,
                                       accum_out=nmx[:, 1, c:c + 1]).then_inc(e_done.sem, 1)

                def evacuate(h):
                    for t in range(NT):
                        wait(act, t_ready, "e", i, hh, h, t)
                        bank, w = (1, 6)[t], of_tile(t, ng)
                        act.activation(eT.rearrange("p m q -> p (m q)")[:, w],
                                       ps[:, bank:bank + 2, :].rearrange("p b n -> p (b n)")[:, 0:w.stop - w.start],
                                       ACT.Copy).then_inc(eT_done.sem, 1)
                exps(0)
                for h in range(HALF):
                    if h + 1 < HALF:
                        exps(h + 1)
                    evacuate(h)

            def half0_out(i):
                act.wait_ge(w_used, ends["y", i] - 8)
                wait(act, o_done, i)
                act.activation(xh[:, 0:4], o, ACT.Copy).then_inc(th_done.sem, 1)

            def stick_half(i, hh):
                def logs(h):
                    wait(act, acc_ready, "z", i, hh, h)
                    if h >= 2:
                        wait(act, sp_done, i, hh, h - 2)
                    w = sw[:, h % 2]
                    own(act.activation(w, zpair(h), ACT.Abs))
                    own(act.activation(w, w, ACT.Exp, scale=-1.0))
                    act.activation(w, w, ACT.Ln, bias=1.0).then_inc(ln_done.sem, 1)

                def weights(h):
                    wait(act, cum_done, i, hh, h)
                    act.activation(sa[:, h % 2], zpair(h), ACT.Exp).then_inc(a_done.sem, 1)
                logs(0)
                logs(1)
                split(1)
                weights(0)
                split(1)
                weights(1)
                logs(2)
                if hh == 0:
                    split(1)
                logs(3)
                if hh == 0:
                    split(1)
                else:
                    half0_out(i)
                weights(2)
                weights(3)

            def mix(l, i):
                kind = mixer_of(l)
                late = []
                for what, hh, g in steps_of(l):
                    if what == "attn":
                        for step in late:
                            copy_t(kind, i, *step)
                        late = []
                        if hh == 1 and kind != "sb":
                            half0_out(i)
                        stick_half(i, hh) if kind == "sb" else softmax_half(kind, i, hh)
                        if (kind, hh) == ("swa", 0):
                            copy_t(kind, i, "q", 1, 0)
                        wait(act, acc_ready, "o", i, hh)
                        if hh == 0:
                            act.activation(o, oall, ACT.Copy).then_inc(o_done.sem, 1)
                        else:
                            act.activation(xh[:, 4:8], oall, ACT.Copy).then_inc(th_done.sem, 1)
                        continue
                    nu = units_of(what)
                    if kind == "sb" and (what, hh) == ("q", 1):
                        late = [(what, hh, g)]
                        continue
                    if kind == "sb" and (what, hh) == ("v", 1):
                        split(1)
                        for step in late:
                            copy_t(kind, i, *step)
                        late = []
                        split(1)
                        continue
                    if kind == "swa":
                        split(nu)
                        if (what, hh) != ("q", 1):
                            late += [(what, hh, g)]
                        continue
                    split(nu - 1)
                    for step in late:
                        copy_t(kind, i, *step)
                    split(1)
                    late = [(what, hh, g)] if what != "v" else []
                split(4)

            def ple(i):
                split(2)
                wait(act, t_ready, "p", i)
                act.activation(pth[:], ps[:, 0, :].rearrange("p (c t m) -> p c t m", c=2, t=NT), ACT.Copy).then_inc(th_done.sem, 1)
                split(4)
                wait(act, acc_ready, "gate", i)
                sigmoid(i, 0)

            def sigmoid(i, t):
                act.activation(eg[:, t, :], ps[:, 4 + 2 * t:6 + 2 * t, :].rearrange("p c n -> p (c n)"),
                               ACT.Sigmoid).then_inc(sig_done.sem, 1)

            split(1)
            stream_t("x", 0, 0)
            split(3)
            stream_t("x", 0, 1)
            for kind, l, i, u0, n in stages:
                assert st["u"] == u0 + LEAD, (kind, st["u"], u0)
                if i == 1:
                    act.wait_ge(c_landed, 16)
                    act.wait_ge(p_landed, 16)
                    act.activation(ident_r[:], ident, ACT.Copy).then_inc(masks_done, 1)
                    act.activation(kill_r[:], const("kill").rearrange("p (b q) -> p b q", b=2), ACT.Copy).then_inc(masks_done, 1)
                if kind in ("ffn1", "ffn2"):
                    act.preload_act_table(ACT.Silu)
                    ffn(i)
                elif kind == "mix":
                    if mixer_of(l) == "sb":
                        act.preload_act_table_set("natural_log_exp_and_others")
                    else:
                        act.preload_act_table(ACT.Exp)
                    mix(l, i)
                else:
                    act.preload_act_table(ACT.Sigmoid)
                    ple(i)
                split(2)
                boundary(kind, i)

        @block.vector
        def _(dve):
            st = {"u": 0, "own": 0}

            def own(ins):
                st["own"] += 1
                ins.then_inc(own_dve, 1)
                dve.wait_ge(own_dve, st["own"])

            after_pool = {u0 + n + LEAD for kind, l, i, u0, n in stages if kind != "ple"}

            def split(n=1, du=0):
                for _ in range(n):
                    u = st["u"]
                    if u >= UNITS:
                        return
                    st["u"] += 1
                    dve.wait_ge(hi_done, u + 1 + du)
                    if u in after_pool:
                        dve.wait_ge(lo_done, u)
                    dve.tensor_tensor(wl[:, u % RING, :], raw[:, u % RING, :], wh[:, u % RING, :].bitcast(F32),
                                      ALU.subtract).then_inc(lo_done, 1)

            def stream_t(key, i, t):
                for c in range(2):
                    wait(dve, th_done, key, i, t, c)
                    dve.tensor_tensor(xl[:, 4 * c:4 * c + 4, t, :], ps[:, 2 * t + c, :].rearrange("p (k m) -> p k m", m=P),
                                      xh[:, 4 * c:4 * c + 4, t, :].bitcast(F32), ALU.subtract).then_inc(tl_done.sem, 1)

            def hidden_t(i, j, n, at, dj=0):
                dve.wait_ge(th_done.sem, th_done.at("h", i, j) + dj)
                for t in range(NT):
                    ins = dve.tensor_tensor(htl[:, at:at + n, t, :], ps[:, 2 + t, 0:n * P].rearrange("p (c m) -> p c m", m=P),
                                            hth[:, at:at + n, t, :].bitcast(F32), ALU.subtract)
                ins.then_inc(tl_done.sem, 1)

            def hidden(i, j, n, dj=0):
                dve.wait_ge(silu_done.sem, silu_done.at(i, j) + dj)
                dve.wait_ge(w_used, ends["up", i, j] + 12 * dj)
                for t in range(NT):
                    ins = dve.scalar_tensor_tensor(hb[:, t, 0:n], sg[:, t, 0:n], 0.5, ps[:, 2 + t, 0:n], ALU.mult, ALU.mult)
                ins.then_inc(h_done.sem, 1)

            def ffn(i):
                split(8)
                hidden(i, 0, BLK)
                with dve.Fori(0, NJ - 1) as r:
                    split(3, r * 12)
                    hidden_t(i, 0, 4, 0, r)
                    split(9, r * 12)
                    hidden(i, 1, BLK, r)
                st["u"] += 12 * (NJ - 2)
                split(2)
                hidden_t(i, NJ - 1, 4, 0)
                split(2)
                hidden(i, NJ, 256)
                split(2)
                hidden_t(i, NJ, 2, 4)

            def y_wait(kind, i, t, c):
                if t == 0:
                    wait(dve, acc_ready, "y", i, c)
                else:
                    dve.wait_ge(w_used, ends["y", i] - (0 if c else 1 if kind == "ple" else 2))

            def residual(kind, i, t, c):
                y_wait(kind, i, t, c)
                h = slice(c * BLK, (c + 1) * BLK)
                return dve.scalar_tensor_tensor(x[:, t, h], x[:, t, h], ALPHA, ps[:, 4 + 2 * t + c, :], ALU.mult, ALU.add,
                                                accum_out=rsum[:, t, c:c + 1])

            def center(i, t, ins):
                own(ins)
                dve.tensor_scalar(nmean[:, t, :], rsum[:, t, 0:1], rsum[:, t, 1:2], -1.0 / D, ALU.add, ALU.mult).then_inc(mean_done.sem, 1)
                wait(dve, mean_done, i, t)
                if t == 0:
                    dve.wait_ge(g_landed, 16 * (norm_index[i] + 1))
                    dve.wait_ge(b_landed, 16 * (norm_index[i] + 1))
                dve.scalar_tensor_tensor(xn[:, t, :], x[:, t, :], nmean[:, t, :], gb[:, 0, :], ALU.add,
                                         ALU.mult).then_inc(xn_done.sem, 1)

            def scale(i, t):
                wait(dve, xn_done, i, t)
                wait(dve, rstd_done, i, t)
                for c in range(2):
                    h = slice(c * BLK, (c + 1) * BLK)
                    dve.scalar_tensor_tensor(x[:, t, h], xn[:, t, h], rstd[:, t, :], gb[:, 1, h], ALU.mult,
                                             ALU.add).then_inc(x_new.sem, 1)

            def embed(i, t):
                for c in range(2):
                    if c == 0:
                        wait(dve, sig_done, i, t)
                    y_wait("ple", i, t, c)
                    h = slice(c * BLK, (c + 1) * BLK)
                    own(dve.tensor_tensor(eg[:, t, h], eg[:, t, h], ps[:, 2 * t + c, :], ALU.mult))
                    dve.tensor_tensor(x[:, t, h], x[:, t, h], eg[:, t, h], ALU.add).then_inc(x_new.sem, 1)

            def boundary(kind, i):
                more = i + 1 < NST
                if kind == "ple":
                    for t in range(NT):
                        embed(i, t)
                        if t == 0:
                            split(2)
                        if more:
                            stream_t("x", i + 1, t)
                    return
                residual(kind, i, 0, 0)
                center(i, 0, residual(kind, i, 0, 1))
                scale(i, 0)
                residual(kind, i, 1, 0)
                stream_t("x", i + 1, 0)
                center(i, 1, residual(kind, i, 1, 1))
                st["u"] += 2
                scale(i, 1)
                stream_t("x", i + 1, 1)

            def rotate(dst, bank, n, cs, t):
                c, s, ns = (const(k)[:, t * 32:(t + 1) * 32].unsqueeze(1).broadcast_to((P, n, 32)) for k in cs)
                v = ps[:, bank, 0:n * HD].rearrange("p (h w d) -> p h w d", w=2, d=32)
                a = ra[:, 0:n * HD].rearrange("p (h w d) -> p h w d", w=2, d=32)
                b = rb[:, 0:n * HD].rearrange("p (h w d) -> p h w d", w=2, d=32)
                for w in range(2):
                    dve.tensor_tensor(a[:, :, w, :], v[:, :, w, :], c, ALU.mult)
                dve.tensor_tensor(b[:, :, 0, :], v[:, :, 1, :], ns, ALU.mult)
                own(dve.tensor_tensor(b[:, :, 1, :], v[:, :, 0, :], s, ALU.mult))
                for d in dst:
                    ins = dve.tensor_tensor(d, ra[:, 0:n * HD].rearrange("p (h d) -> p h d", d=HD),
                                            rb[:, 0:n * HD].rearrange("p (h d) -> p h d", d=HD), ALU.add)
                own(ins)
                return ins

            def tokens(kind, what, i, hh, g):
                dve.wait_ge(w_used, ends[what, i, hh, g])
                pair = bank_of(kind, what, hh)
                if what in ("q", "k", "kv"):
                    for t in range(NT):
                        if kind == "sb":
                            if what == "q":
                                ins = dve.tensor_scalar(qk[:, t, :], ps[:, pair + t, :], HD ** -0.5, None, ALU.mult)
                            else:
                                ins = dve.tensor_copy(qk[:, t, :], ps[:, pair + t, :])
                        elif what == "kv":
                            d = kvt[:, t, :].rearrange("p (h w d) -> p h w d", h=2, w=2)
                            rotate([d[:, :, 0, :], d[:, :, 1, :]], pair + t, 2, ("ck", "sk", "nsk"), t)
                        else:
                            rotate([qk[:, t, :].rearrange("p (h d) -> p h d", d=HD)], pair + t, 8,
                                   ("cq", "sq", "nsq") if what == "q" else ("ck", "sk", "nsk"), t)
                    if kind == "sb":
                        ins.then_inc(tok_done.sem, 1)
                    else:
                        dve.sem_inc(tok_done.sem, 1)
                if what == "v":
                    ins = dve.tensor_copy(vv[:, g, :, :], ps[:, pair:pair + 2, :])
                    ins.then_inc(v_done.sem, 1)
                if what == "kv":
                    ins = dve.tensor_copy(vv[:, 0, :, 0:P], ps[:, pair:pair + 2, P:2 * P])
                    ins.then_inc(v_done.sem, 1)

            def softmax_half(kind, i, hh):
                ng = NG if kind == "dil" else 1

                def scores(h):
                    for t in range(NT):
                        wait(dve, acc_ready, "z", i, hh, h, t)
                        if h >= 3:
                            wait(dve, t_ready, "e", i, hh, h - 3, t)
                        w = of_tile(t, ng)
                        bank = (0, 4)[t]
                        z = ps[:, bank:bank + 2, :].rearrange("p b n -> p (b n)")[:, 0:w.stop - w.start]
                        low = nsink[:, hh * HALF + h:hh * HALF + h + 1] if kind == "swa" else -NEG
                        dve.tensor_tensor_reduce(sc[:, h % 3, w], z, const(kind)[:, w], -1.0, low, ALU.add, ALU.min,
                                                 nmx[:, 0, 2 * h + t:2 * h + t + 1]).then_inc(s_done.sem, 1)

                def normalize(h):
                    both = slice(2 * h, 2 * h + 2)
                    wait(dve, e_done, i, hh, h, 1)
                    if kind == "swa":
                        own(dve.tensor_tensor(nmx[:, 1, both], nmx[:, 1, both], nmx[:, 2, both], ALU.add))
                    own(dve.reciprocal(nmx[:, 3, both], nmx[:, 1, both]))
                    for t in range(NT):
                        w = of_tile(t, ng)
                        dve.tensor_scalar(sc[:, h % 3, w], sc[:, h % 3, w], nmx[:, 3, 2 * h + t:2 * h + t + 1], None,
                                          ALU.mult).then_inc(p_done.sem, 1)
                scores(0)
                scores(1)
                for h in range(HALF):
                    normalize(h)
                    if h + 2 < HALF:
                        scores(h + 2)

            def half0_out(i):
                wait(dve, th_done, "o", i, 0)
                dve.tensor_tensor(xl[:, 0:4], o, xh[:, 0:4].bitcast(F32), ALU.subtract).then_inc(tl_done.sem, 1)

            def stick_half(i, hh):
                def soft(h):
                    wait(dve, ln_done, i, hh, h)
                    dve.scalar_tensor_tensor(ssp[:, h % 2], zpair(h), 0.0, sw[:, h % 2], ALU.max, ALU.add).then_inc(sp_done.sem, 1)
                soft(0)
                soft(1)
                split(2)
                if hh == 1:
                    tokens("sb", "v", i, 1, 0)
                soft(2)
                if hh == 0:
                    split(1)
                soft(3)
                if hh == 0:
                    split(1)
                else:
                    half0_out(i)

            def mix(l, i):
                kind = mixer_of(l)
                for what, hh, g in steps_of(l):
                    if what == "attn":
                        if hh == 1 and kind != "sb":
                            half0_out(i)
                        stick_half(i, hh) if kind == "sb" else softmax_half(kind, i, hh)
                        if hh == 1:
                            wait(dve, th_done, "o", i, 1)
                            dve.tensor_tensor(xl[:, 4:8], oall, xh[:, 4:8].bitcast(F32), ALU.subtract).then_inc(tl_done.sem, 1)
                        continue
                    if kind == "sb" and (what, hh) == ("v", 1):
                        split(2)
                        continue
                    if not (kind == "sb" and (what, hh) == ("q", 1)):
                        split(units_of(what))
                    tokens(kind, what, i, hh, g)
                split(4)

            def ple(i):
                split(2)
                wait(dve, th_done, "p", i)
                dve.tensor_tensor(ptl[:], ps[:, 0, :].rearrange("p (c t m) -> p c t m", c=2, t=NT), pth[:].bitcast(F32),
                                  ALU.subtract).then_inc(tl_done.sem, 1)
                split(4)

            split(1)
            stream_t("x", 0, 0)
            split(3)
            stream_t("x", 0, 1)
            for kind, l, i, u0, n in stages:
                assert st["u"] == u0 + LEAD, (kind, st["u"], u0)
                if i == 1:
                    dve.wait_ge(c_landed, 16)
                    dve.wait_ge(p_landed, 16)
                    own(dve.tensor_scalar(nsink[:], const("sink"), -1.0, None, ALU.mult))
                if kind in ("ffn1", "ffn2"):
                    ffn(i)
                elif kind == "mix":
                    mix(l, i)
                else:
                    ple(i)
                split(2)
                boundary(kind, i)

        @block.tensor
        def _(pe):
            st = {"u": 0}

            def three(out_, a_h, a_l, u, k, ncol, start, stop, cols=None):
                b_h = view(wh, u % RING, ncol)[:, k, :]
                b_l = view(wl, u % RING, ncol)[:, k, :]
                pe.matmul(out_, a_h, b_h, start=start, stop=False)
                pe.matmul(out_, a_h, b_l, start=False, stop=False)
                return pe.matmul(out_, a_l, b_h, start=False, stop=stop)

            def unit(u, t, bank, chunk0, ncol, ah, al, start, stop):
                nk = UW // ncol
                for k in range(nk):
                    ins = three(ps[:, bank, 0:ncol], ah[:, chunk0 + k, t, :], al[:, chunk0 + k, t, :], u, k, ncol,
                                start and k == 0, stop and k == nk - 1)
                return ins

            def ready(u, du=0):
                pe.wait_ge(lo_done, u + 1 + du)

            def run(items, by_tile, du=0, y=(), before=None):
                u = st["u"]
                st["u"] += len(items)
                if by_tile:
                    for t in range(NT):
                        for n, it in enumerate(items):
                            if before:
                                before(t, n)
                            if t == 0:
                                ready(u + n, du)
                            ins = unit(u + n, t, *it(t))
                            if t == NT - 1:
                                ins.then_inc(w_used, 1)
                            elif n in y:
                                ins.then_inc(acc_ready.sem, 1)
                else:
                    for n, it in enumerate(items):
                        ready(u + n, du)
                        for t in range(NT):
                            if before:
                                before(t, n)
                            ins = unit(u + n, t, *it(t))
                        ins.then_inc(w_used, 1)

            def transposes(src, n, bank, t, at=0):
                for c in range(n):
                    ins = pe.transpose(ps[:, bank + c // 4, (c % 4) * P:(c % 4 + 1) * P], src[:, at + c * P:at + (c + 1) * P], ident)
                return ins

            def stream_t(key, i, t):
                for c in range(2):
                    if i:
                        wait(pe, x_new, i - 1, t, c)
                    else:
                        pe.wait_ge(x_landed[t], 16)
                    transposes(x[:, t, :], 4, 2 * t + c, t, c * BLK).then_inc(t_ready.sem, 1)

            def y_items(nunits, ah, al, banks=lambda t, c: 4 + 2 * t + c, n0=0, chunk0=0, first=True, last=True):
                items = []
                for n in range(nunits):
                    k, c = n // 2, n % 2
                    items.append(lambda t, k=k, c=c: (banks(t, c), chunk0 + 2 * k, BLK, ah, al, first and k == 0,
                                                      last and k == nunits // 2 - 1))
                return items

            def col_items(pair, ncol, ah=xh, al=xl):
                nk = UW // ncol
                n = 8 // nk
                return [lambda t, m=m: (pair + t, m * nk, ncol, ah, al, m == 0, m == n - 1) for m in range(n)]

            def hidden_t(i, j, n, dj=0):
                pe.wait_ge(h_done.sem, h_done.at(i, j) + dj)
                for t in range(NT):
                    ins = transposes(hb[:, t, :], n, 2 + t, t)
                ins.then_inc(t_ready.sem, 1)

            def opening(i, half1):
                def f(t, n):
                    if n == 0:
                        wait(pe, tl_done, "x", i, t, 0)
                    if n == half1:
                        wait(pe, tl_done, "x", i, t, 1)
                    if (t, n) == (0, 3):
                        stream_t("x", i, 1)
                return f

            def closing(i, more=None):
                def f(t, n):
                    if more:
                        more(t, n)
                    if (t, n) == (1, 3) and i + 1 < NST:
                        stream_t("x", i + 1, 0)
                return f

            def ffn(i):
                run(col_items(0, BLK), True, before=opening(i, 2))
                run(col_items(2, BLK), False)
                def block_of(j, dj, first):
                    du = 12 * dj
                    g = col_items(0, BLK)
                    pe.wait_ge(silu_done.sem, silu_done.at(i, j - 1) + dj)
                    run(g[0:3], False, du=du)
                    hidden_t(i, j - 1, 4, dj)
                    run(g[3:4], False, du=du)
                    pe.wait_ge(tl_done.sem, tl_done.at("h", i, j - 1) + dj)
                    run(y_items(4, hth, htl, first=first, last=False), False, du=du)
                    run(col_items(2, BLK), False, du=du)

                block_of(1, 0, True)
                with pe.Fori(0, NJ - 2) as r:
                    block_of(2, r, False)
                st["u"] += 12 * (NJ - 3)
                g = col_items(0, 256)
                wait(pe, silu_done, i, NJ - 1)
                run(g[0:1], False)
                hidden_t(i, NJ - 1, 4)
                run(g[1:2], False)
                wait(pe, tl_done, "h", i, NJ - 1)
                run(col_items(2, 256), False)
                down = y_items(4, hth, htl, first=False, last=False)
                run(down[0:1], False)
                hidden_t(i, NJ, 2)
                run(down[1:2], False)
                last = y_items(2, hth, htl, chunk0=4, first=False)
                run([down[2], last[0], down[3], last[1]], True, y=(1, 3),
                    before=closing(i, lambda t, n: wait(pe, tl_done, "h", i, NJ) if (t, n) == (0, 1) else None))

            def attn_z(i, hh, h, t, ng, kc):
                pb = HD * (h % 2)
                for g in range(ng):
                    bank = 0 if t == 0 else 4 + (g * 256) // BLK
                    at = (g * (t + 1) * P) % BLK
                    ins = pe.matmul(ps[:, bank, at:at + (t + 1) * P],
                                    qT[pb:pb + HD, g if kc is None else hh, h // 2, t * P:(t + 1) * P],
                                    kT[pb:pb + HD, g, h // 2 if kc is None else kc, 0:(t + 1) * P], start=True, stop=True)
                ins.then_inc(acc_ready.sem, 1)

            def softmax_half(kind, i, hh, v_key):
                ng = NG if kind == "dil" else 1
                kc = None if kind == "dil" else hh

                def z(h):
                    for t in range(NT):
                        if h:
                            wait(pe, s_done, i, hh, h - 1, t)
                        attn_z(i, hh, h, t, ng, kc)

                def tr(h):
                    for t in range(NT):
                        wait(pe, p_done, i, hh, h, t)
                        transposes(sc[:, h % 3, of_tile(t, ng)], ng * (t + 1), (1, 6)[t], t).then_inc(t_ready.sem, 1)
                    if (kind, hh, h) == ("swa", 0, HALF - 1):
                        head_t(kind, i, "q", 1, 0)

                def av(h):
                    for t in range(NT):
                        wait(pe, eT_done, i, hh, h, t)
                        m, n = 0, ng * (t + 1)
                        for g in range(ng):
                            for kb in range(t + 1):
                                v = vv[:, g, kb, h * HD:(h + 1) * HD] if kind == "dil" else vv[:, 0, kb, hh * HD:(hh + 1) * HD]
                                pb = HD * (h % 2)
                                ins = pe.matmul(opair(h)[pb:pb + HD, t * P:(t + 1) * P], v, eT[:, t * ng + m, :],
                                                start=m == 0, stop=m == n - 1)
                                m += 1
                    return ins
                z(0)
                z(1)
                wait(pe, v_done, *v_key)
                if kind == "swa":
                    wait(pe, tok_done, "q", i, 1, 0)
                if hh == 1:
                    wait(pe, o_done, i)
                for h in range(HALF):
                    if h:
                        av(h - 1)
                    tr(h)
                    if h + 2 < HALF:
                        z(h + 2)
                av(HALF - 1).then_inc(acc_ready.sem, 1)

            def stick_half(i, hh, filler, v_key):
                def z(h):
                    for m in range(2):
                        pb = HD * m
                        q, k = qT[pb:pb + HD, 0, h, :], kT[pb:pb + HD, 0, h, :]
                        pe.matmul(zpair(h)[:, m, 0:S], k[:, 0:P], q, start=True, stop=False)
                        pe.matmul(zpair(h)[:, m, S:S + P], k[:, P:S], q[:, P:S], start=False, stop=False)
                        ins = pe.matmul(zpair(h)[:, m, :].rearrange("p (b q) -> p b q", q=P)[:, 0:3:2, :], ident_r[:], kill_r[:],
                                        start=False, stop=True)
                    ins.then_inc(acc_ready.sem, 1)

                def cum(h):
                    wait(pe, sp_done, i, hh, h)
                    for m in range(2):
                        pe.matmul(zpair(h)[:, m, :], const("lower"), ssp[:, h % 2, m, :], start=False, stop=False, skip_group_check=True)
                        ins = pe.matmul(zpair(h)[:, m, P:2 * P], const("ones"), ssp[:, h % 2, m, 2 * P:3 * P], start=False,
                                        stop=True, skip_group_check=True)
                    ins.then_inc(cum_done.sem, 1)

                def av(h):
                    wait(pe, a_done, i, hh, h)
                    for m in range(2):
                        a = sa[:, h % 2, m, :]
                        c = slice((2 * h + m) * HD, (2 * h + m + 1) * HD)
                        out_ = opair(2 * h)[HD * m:HD * (m + 1), :]
                        pe.matmul(out_, vv[:, 0, 0, c], a[:, 0:S], start=True, stop=False)
                        ins = pe.matmul(out_[:, P:S], vv[:, 0, 1, c], a[:, S:S + P], start=False, stop=True)
                    return ins

                def fill(h):
                    run(filler[h:h + 1], False)
                if hh == 0:
                    pe.wait_ge(masks_done, 2)
                z(0)
                if hh == 0:
                    wait(pe, v_done, *v_key)
                z(1)
                fill(0)
                cum(0)
                fill(1)
                cum(1)
                if hh == 1:
                    wait(pe, v_done, *v_key)
                av(0)
                z(2)
                fill(2)
                av(1)
                z(3)
                cum(2)
                fill(3)
                cum(3)
                av(2)
                av(3).then_inc(acc_ready.sem, 1)

            def head_t(kind, i, what, hh, g):
                wait(pe, tok_done, what, i, hh, g)
                for t in range(NT):
                    ins = transposes((kvt if what == "kv" else qk)[:, t, :], 2 if what == "kv" else 4, 4 + t, t)
                ins.then_inc(t_ready.sem, 1)

            def mix_swa(l, i):
                run(col_items(bank_of("swa", "q", 0), BLK), True, before=opening(i, 2))
                run(col_items(bank_of("swa", "kv", 0), 256), False)
                items = col_items(bank_of("swa", "q", 1), BLK)
                run(items[0:2], False)
                head_t("swa", i, "q", 0, 0)
                run(items[2:3], False)
                wait(pe, th_done, "q", i, 0, 0)
                head_t("swa", i, "kv", 0, 0)
                run(items[3:4], False)
                wait(pe, th_done, "kv", i, 0, 0)
                softmax_half("swa", i, 0, (i, 0, 0))
                wait(pe, th_done, "q", i, 1, 0)
                softmax_half("swa", i, 1, (i, 0, 0))
                project_out(i)

            def project_out(i):
                wait(pe, tl_done, "o", i, 0)
                y = y_items(8, xh, xl)
                run(y[0:4], False)
                wait(pe, tl_done, "o", i, 1)
                run([y[4], y[6], y[5], y[7]], True, y=(1, 3), before=closing(i))

            def mix(l, i):
                kind = mixer_of(l)
                if kind == "swa":
                    return mix_swa(l, i)
                pending = None
                steps = steps_of(l)

                first = True
                filled = False
                used = {}
                copied = None
                for what, hh, g in steps:
                    if (kind, what, hh) == ("sb", "v", 1):
                        vitems = col_items(bank_of(kind, what, hh), BLK)
                        wait(pe, th_done, *copied)
                        run(vitems[0:1], False)
                        head_t(kind, i, *pending)
                        copied = (pending[0], i, pending[1], pending[2])
                        pending = None
                        run(vitems[1:2], False)
                        continue
                    if what == "attn":
                        if pending:
                            if copied:
                                wait(pe, th_done, *copied)
                            head_t(kind, i, *pending)
                            copied = (pending[0], i, pending[1], pending[2])
                            pending = None
                        wait(pe, th_done, *copied)
                        v_key = i, hh, NG - 1 if kind == "dil" else 0
                        used = {}
                        if kind == "sb":
                            stick_half(i, hh, col_items(0, BLK) if hh == 0 else vitems[2:4], v_key)
                            if hh == 0:
                                used[0], pending, filled = ("q", i, 1, 0), ("q", 1, 0), True
                        else:
                            softmax_half(kind, i, hh, v_key)
                        continue
                    if filled:
                        filled = False
                        continue
                    pair = bank_of(kind, what, hh)
                    if pair == 2 and hh == 1 and g == 0:
                        if pending and kind == "sb":
                            head_t(kind, i, *pending)
                            copied = (pending[0], i, pending[1], pending[2])
                            pending = None
                        wait(pe, o_done, i)
                    if pair in used:
                        if pair == 6:
                            wait(pe, v_done, *used[pair])
                        else:
                            wait(pe, tok_done, *used[pair])
                    used[pair] = (i, hh, g) if what == "v" else (what, i, hh, g)
                    items = col_items(pair, BLK)
                    if first:
                        run(items, True, before=opening(i, 2))
                        first = False
                    else:
                        run(items[:-1], False)
                        if pending:
                            if copied:
                                wait(pe, th_done, *copied)
                            head_t(kind, i, *pending)
                            copied = (pending[0], i, pending[1], pending[2])
                            pending = None
                        run(items[-1:], False)
                    if what != "v":
                        pending = (what, hh, g)
                project_out(i)

            def ple(l, i):
                y = y_items(8, xh, xl)
                run(y[0:4], True, before=opening(i, 4))
                pe.wait_ge(p_landed, 16 * (l + 2))
                for t in range(NT):
                    for c in range(2):
                        ins = pe.transpose(ps[:, 0, (2 * c + t) * P:(2 * c + t + 1) * P], pin[:, t, c * P:(c + 1) * P], ident)
                ins.then_inc(t_ready.sem, 1)
                wait(pe, tl_done, "x", i, 1, 1)
                run(y[4:6], False)
                pr = y_items(2, pth, ptl, banks=lambda t, c: 2 * t + c)
                wait(pe, tl_done, "p", i)
                run(y[6:8] + pr, True, y=(1, 2, 3), before=closing(i))

            pe.wait_ge(i_landed, 16)
            stream_t("x", 0, 0)
            for kind, l, i, u0, n in stages:
                if i == 1:
                    pe.wait_ge(c_landed, 16)
                assert st["u"] == u0, (kind, st["u"], u0)
                if kind in ("ffn1", "ffn2"):
                    ffn(i)
                elif kind == "mix":
                    mix(l, i)
                else:
                    ple(l, i)


def constants():
    import numpy as np
    t = np.zeros((P, CONST["sink"][0]), np.float32)

    def put(name, v):
        a, b = CONST[name]
        t[:, a:b] = v
    p, q = np.arange(P)[:, None], np.arange(P)[None, :]
    put("ident", p == q)
    put("lower", -1.0 * (p >= q))
    put("ones", -1.0)
    kill = np.where(p < q, 0.0, NEG)
    put("kill", np.concatenate([kill, kill], 1))
    key = np.arange(S)[None, :]

    def banded(ok):
        return [np.where(ok(t * P + p - key[:, 0:(t + 1) * P]), 0.0, NEG) for t in range(NT)]
    put("swa", np.concatenate(banded(lambda d: (d >= 0) & (d <= 127)), 1))
    per = [banded(lambda d, w=w, s=s: (d >= 0) & (d % s == 0) & (d // s <= w // s)) for w, s in DIL]
    put("dil", np.concatenate([m[t] for t in range(NT) for m in per], 1))
    pos = np.arange(S, dtype=np.float32)
    inv = np.float32(10000.0) ** (-np.arange(0, HD, 2, dtype=np.float32) / np.float32(HD))
    ang = (pos[:, None] * inv[None, :]).astype(np.float32)
    c, s = np.cos(ang), np.sin(ang)
    rows = lambda m: np.concatenate([m[0:P], m[P:S]], 1)
    for name, m in (("cq", c * HD ** -0.5), ("sq", s * HD ** -0.5), ("nsq", -s * HD ** -0.5), ("ck", c), ("sk", s), ("nsk", -s)):
        put(name, rows(m))
    return t


_INS = ['x', 'p', 'ffn1_w_in', 'ffn1_w_out', 'ffn2_w_in', 'ffn2_w_out', 'ln_g', 'ln_b', 'sb_w_in', 'sb_w_out',
        'swa_w_in', 'swa_sinks', 'swa_w_out', 'dil_w_in', 'dil_w_out', 'ple_w_proj', 'ple_w_gate']


def kernel(**inputs):
    import numpy as np
    import concourse.bacc as bacc
    from concourse.bass_utils import run_bass_kernel_spmd

    nc = bacc.Bacc("TRN2", target_bir_lowering=False, num_devices=1)
    arrays, aps = {}, {}
    for name in _INS:
        arrays[f"in_{name}"] = np.ascontiguousarray(inputs[name])
    arrays["in_consts"] = constants()
    for name in _INS + ["consts"]:
        a = arrays[f"in_{name}"]
        aps[name] = nc.dram_tensor(f"in_{name}", a.shape, mybir.dt.from_np(a.dtype), kind="ExternalInput").ap()
    out = nc.dram_tensor("out_dram", (1, S, D), F32, kind="ExternalOutput").ap()
    build_program(nc, aps, out)
    r = run_bass_kernel_spmd(nc, [arrays], core_ids=[0])
    return r.results[0]["out_dram"]
```
